# Optimizing a Trainium2 kernel written in Bass

```python
import math
import jax, jax.numpy as jnp
from jax import lax
import numpy as np

D_MODEL = 1024
BATCH = 1
SEQ = 256
DEPTH = 2

HEAD_DIM = 64
ROPE_THETA = 500000.0
ROPE_FRAC = 4
EPS = 1e-6
Q_BLOCK = 128

A_WIDTH = D_MODEL // 2
A_GROUPS = 4
A_GDIM = A_WIDTH // A_GROUPS
A_CHUNK = 128

B_HEADS = 8
B_QK_DIM = 32
B_V_DIM = 2 * B_QK_DIM
B_WIDTH = B_HEADS * B_V_DIM

C_WIDTH = D_MODEL // 2
C_KERNEL = 31

D_HEADS = 8
D_KV_GROUPS = 2
D_WIDTH = D_HEADS * HEAD_DIM
CMP_BLOCK = 32
CMP_STRIDE = 16
CMP_HIDDEN = 2 * HEAD_DIM
SLC_BLOCK = 64
SLC_TOPK = 16
WINDOW = 512

MEM_TOKENS = 256
M_HEADS = 4
M_WIDTH = M_HEADS * HEAD_DIM

MIX_WIDTH = A_WIDTH + B_WIDTH + M_WIDTH
EVEN_SPLITS = (A_WIDTH, A_WIDTH, A_WIDTH,
               2 * B_HEADS * B_QK_DIM, 2 * B_HEADS * B_QK_DIM, B_WIDTH, B_WIDTH,
               M_WIDTH, M_WIDTH)
ODD_SPLITS = (C_WIDTH, C_WIDTH, C_WIDTH,
              D_WIDTH, 6 * D_KV_GROUPS * HEAD_DIM, 3 * D_HEADS, D_WIDTH,
              M_WIDTH, M_WIDTH)
EVEN_IN = sum(EVEN_SPLITS)
ODD_IN = sum(ODD_SPLITS)


def rms_norm(x, g):
    xf = x.astype(jnp.float32)
    y = xf * lax.rsqrt(jnp.mean(xf * xf, axis=-1, keepdims=True) + EPS)
    return (y * g.astype(jnp.float32)).astype(x.dtype)

def rope_partial(x, pos):
    d = x.shape[-1]
    rd = d // ROPE_FRAC
    half = rd // 2
    inv = ROPE_THETA ** (-jnp.arange(half, dtype=jnp.float32) / half)
    ang = pos.astype(jnp.float32)[:, None] * inv[None, :]
    cos = jnp.cos(ang).astype(x.dtype)
    sin = jnp.sin(ang).astype(x.dtype)
    x1, x2, rest = x[..., :half], x[..., half:rd], x[..., rd:]
    return jnp.concatenate([x1 * cos - x2 * sin, x1 * sin + x2 * cos, rest], axis=-1)

def masked_softmax(s, mask):
    s = jnp.where(mask, s, -jnp.inf)
    m = jnp.max(s, axis=-1, keepdims=True)
    m = jnp.where(jnp.isfinite(m), m, 0.0)
    e = jnp.where(mask, jnp.exp(s - m), 0.0)
    return e / jnp.maximum(jnp.sum(e, axis=-1, keepdims=True), jnp.finfo(jnp.float32).tiny)

def split_cols(x, sizes):
    return jnp.split(x, [int(v) for v in np.cumsum(sizes)[:-1]], axis=-1)

def chunked_sgu(u, v, w_s, b_s, v_gain):
    Bz, S, _ = v.shape
    v = rms_norm(v.reshape(Bz, S, A_GROUPS, A_GDIM), v_gain.reshape(A_GROUPS, A_GDIM))
    v = v.reshape(Bz, S // A_CHUNK, A_CHUNK, A_GROUPS, A_GDIM)
    causal = jnp.tril(jnp.ones((A_CHUNK, A_CHUNK), dtype=bool))
    w = jnp.where(causal[None], w_s, 0.0)
    z = jnp.einsum('gts,bcsgd->bctgd', w, v) + b_s.T[:, :, None]
    return u * z.reshape(Bz, S, A_WIDTH)

def diff_attention(q, k, v, lam):
    Bz, H, _, S, dk = q.shape
    dv = v.shape[-1]
    nblk = S // Q_BLOCK
    scale = dk ** -0.5
    kpos = jnp.arange(S)
    qb = q.reshape(Bz, H, 2, nblk, Q_BLOCK, dk).transpose(3, 0, 1, 2, 4, 5)

    def block(args):
        qi, c = args
        qpos = c * Q_BLOCK + jnp.arange(Q_BLOCK)
        s = jnp.einsum('bhmqd,bhmkd->bhmqk', qi, k).astype(jnp.float32) * scale
        s = jnp.where(kpos[None, :] <= qpos[:, None], s, -jnp.inf)
        p = jax.nn.softmax(s, axis=-1)
        pd = p[:, :, 0] - lam * p[:, :, 1]
        return jnp.einsum('bhqk,bhkd->bhqd', pd.astype(v.dtype), v)

    o = lax.map(block, (qb, jnp.arange(nblk)))
    return o.transpose(1, 0, 3, 2, 4).reshape(Bz, S, H, dv)

def memory_attention(q, mem_n, w_kv, qnorm, knorm):
    Bz, S, _ = q.shape
    k, v = jnp.split(mem_n @ w_kv, 2, axis=-1)
    q = rms_norm(q.reshape(Bz, S, M_HEADS, HEAD_DIM), qnorm)
    k = rms_norm(k.reshape(Bz, -1, M_HEADS, HEAD_DIM), knorm)
    v = v.reshape(Bz, -1, M_HEADS, HEAD_DIM)
    s = jnp.einsum('bshd,bmhd->bhsm', q, k).astype(jnp.float32) * (HEAD_DIM ** -0.5)
    p = jax.nn.softmax(s, axis=-1)
    return jnp.einsum('bhsm,bmhd->bshd', p.astype(v.dtype), v).reshape(Bz, S, M_WIDTH)

def conformer_conv(a, b, conv_w, conv_b, norm_g):
    h = a * jax.nn.sigmoid(b)
    hp = jnp.pad(h, ((0, 0), (C_KERNEL - 1, 0), (0, 0)))
    y = lax.conv_general_dilated(hp, conv_w[:, None, :], window_strides=(1,), padding='VALID',
                                 dimension_numbers=('NWC', 'WIO', 'NWC'),
                                 feature_group_count=C_WIDTH) + conv_b
    return jax.nn.silu(rms_norm(y, norm_g))

def compress(t, cmp_idx, pos_emb, w1, w2):
    Bz, _, G, hd = t.shape
    blocks = t[:, cmp_idx] + pos_emb[:, None, :]
    flat = blocks.transpose(0, 1, 3, 2, 4).reshape(Bz, cmp_idx.shape[0], G, CMP_BLOCK * hd)
    return jax.nn.silu(flat @ w1) @ w2

def cmp_to_slc_overlap(n_cmp, n_slc):
    start = np.arange(n_cmp) * CMP_STRIDE
    s0 = np.arange(n_slc) * SLC_BLOCK
    lo = np.maximum(start[:, None], s0[None, :])
    hi = np.minimum(start[:, None] + CMP_BLOCK, s0[None, :] + SLC_BLOCK)
    return (np.clip(hi - lo, 0, None) / CMP_BLOCK).astype(np.float32)

def nsa(q, kv, gates, pos, qnorm, knorm, cmp_pos_k, cmp_w1_k, cmp_w2_k,
        cmp_pos_v, cmp_w1_v, cmp_w2_v):
    Bz, S = q.shape[:2]
    G, R, hd = D_KV_GROUPS, D_HEADS // D_KV_GROUPS, HEAD_DIM
    nblk = S // Q_BLOCK
    n_cmp = (S - CMP_BLOCK) // CMP_STRIDE + 1
    n_slc = S // SLC_BLOCK
    n_sel = min(SLC_TOPK, n_slc)
    scale = hd ** -0.5

    q = rope_partial(rms_norm(q, qnorm).transpose(0, 2, 1, 3), pos).reshape(Bz, G, R, S, hd)
    k_cmp_raw, v_cmp_raw, k_slc, v_slc, k_win, v_win = [kv[:, :, i] for i in range(6)]

    cmp_idx = np.arange(n_cmp)[:, None] * CMP_STRIDE + np.arange(CMP_BLOCK)[None, :]
    cmp_end = jnp.asarray(cmp_idx[:, -1])
    kc = compress(k_cmp_raw, cmp_idx, cmp_pos_k, cmp_w1_k, cmp_w2_k)
    vc = compress(v_cmp_raw, cmp_idx, cmp_pos_v, cmp_w1_v, cmp_w2_v).transpose(0, 2, 1, 3)
    kc = rope_partial(rms_norm(kc, knorm).transpose(0, 2, 1, 3), cmp_end)

    ks = rope_partial(rms_norm(k_slc, knorm).transpose(0, 2, 1, 3), pos)
    kb = ks.reshape(Bz, G, n_slc, SLC_BLOCK, hd)
    vb = v_slc.transpose(0, 2, 1, 3).reshape(Bz, G, n_slc, SLC_BLOCK, hd)

    pad = ((0, 0), (0, 0), (WINDOW, 0), (0, 0))
    kw = jnp.pad(rope_partial(rms_norm(k_win, knorm).transpose(0, 2, 1, 3), pos), pad)
    vw = jnp.pad(v_win.transpose(0, 2, 1, 3), pad)

    overlap = jnp.asarray(cmp_to_slc_overlap(n_cmp, n_slc))
    b_ix = jnp.arange(Bz)[:, None, None, None]
    g_ix = jnp.arange(G)[None, :, None, None]
    blk_tok = jnp.arange(SLC_BLOCK)
    slc_ids = jnp.arange(n_slc)
    win_off = jnp.arange(WINDOW + Q_BLOCK) - WINDOW

    qb = q.reshape(Bz, G, R, nblk, Q_BLOCK, hd).transpose(3, 0, 1, 2, 4, 5)
    gb = gates.transpose(0, 2, 1, 3).reshape(Bz, G, R, nblk, Q_BLOCK, 3).transpose(3, 0, 1, 2, 4, 5)

    def block(args):
        qi, gt, c = args
        qpos = c * Q_BLOCK + jnp.arange(Q_BLOCK)
        s = jnp.einsum('bgrqd,bgnd->bgrqn', qi, kc).astype(jnp.float32) * scale
        p_c = masked_softmax(s, cmp_end[None, :] <= qpos[:, None])
        o_c = jnp.einsum('bgrqn,bgnd->bgrqd', p_c.astype(vc.dtype), vc)
        imp = jnp.einsum('bgrqn,nj->bgqj', p_c, overlap)
        cur = (qpos // SLC_BLOCK)[:, None]
        imp = jnp.where(slc_ids[None, :] > cur, -jnp.inf, imp)
        forced = (slc_ids[None, :] == 0) | (slc_ids[None, :] == cur) | (slc_ids[None, :] == cur - 1)
        imp = jnp.where(forced, jnp.inf, imp)
        _, sel = lax.top_k(imp, n_sel)
        ksel = kb[b_ix, g_ix, sel].reshape(Bz, G, Q_BLOCK, n_sel * SLC_BLOCK, hd)
        vsel = vb[b_ix, g_ix, sel].reshape(Bz, G, Q_BLOCK, n_sel * SLC_BLOCK, hd)
        kpos = (sel[..., None] * SLC_BLOCK + blk_tok).reshape(Bz, G, Q_BLOCK, n_sel * SLC_BLOCK)
        s = jnp.einsum('bgrqd,bgqkd->bgrqk', qi, ksel).astype(jnp.float32) * scale
        p_s = masked_softmax(s, (kpos <= qpos[:, None])[:, :, None])
        o_s = jnp.einsum('bgrqk,bgqkd->bgrqd', p_s.astype(vsel.dtype), vsel)
        kwi = lax.dynamic_slice_in_dim(kw, c * Q_BLOCK, WINDOW + Q_BLOCK, axis=2)
        vwi = lax.dynamic_slice_in_dim(vw, c * Q_BLOCK, WINDOW + Q_BLOCK, axis=2)
        wpos = c * Q_BLOCK + win_off
        dpos = qpos[:, None] - wpos[None, :]
        s = jnp.einsum('bgrqd,bgkd->bgrqk', qi, kwi).astype(jnp.float32) * scale
        p_w = masked_softmax(s, (wpos[None, :] >= 0) & (dpos >= 0) & (dpos < WINDOW))
        o_w = jnp.einsum('bgrqk,bgkd->bgrqd', p_w.astype(vwi.dtype), vwi)
        return gt[..., 0:1] * o_c + gt[..., 1:2] * o_s + gt[..., 2:3] * o_w

    o = lax.map(block, (qb, gb, jnp.arange(nblk)))
    return o.transpose(1, 0, 4, 2, 3, 5).reshape(Bz, S, D_WIDTH)

def even_layer(x, mem_n, pos, layer, norm_g, w_in, a_vnorm, a_ws, a_bs, b_qnorm, b_knorm,
               b_lq1, b_lk1, b_lq2, b_lk2, b_subln, m_wkv, m_qnorm, m_knorm, w_out):
    Bz, S, _ = x.shape
    h = rms_norm(x, norm_g)
    a_u, a_v, a_g, b_q, b_k, b_v, b_g, m_q, m_g = split_cols(h @ w_in, EVEN_SPLITS)
    y_a = chunked_sgu(jax.nn.gelu(a_u), jax.nn.gelu(a_v), a_ws, a_bs, a_vnorm) * jax.nn.silu(a_g)
    lam_init = 0.8 - 0.6 * math.exp(-0.3 * layer)
    lam = (jnp.exp(jnp.sum(b_lq1.astype(jnp.float32) * b_lk1.astype(jnp.float32)))
           - jnp.exp(jnp.sum(b_lq2.astype(jnp.float32) * b_lk2.astype(jnp.float32))) + lam_init)
    q = rms_norm(b_q.reshape(Bz, S, B_HEADS, 2, B_QK_DIM), b_qnorm).transpose(0, 2, 3, 1, 4)
    k = rms_norm(b_k.reshape(Bz, S, B_HEADS, 2, B_QK_DIM), b_knorm).transpose(0, 2, 3, 1, 4)
    q, k = rope_partial(q, pos), rope_partial(k, pos)
    v = b_v.reshape(Bz, S, B_HEADS, B_V_DIM).transpose(0, 2, 1, 3)
    o_b = rms_norm(diff_attention(q, k, v, lam), b_subln) * (1.0 - lam_init)
    y_b = o_b.reshape(Bz, S, B_WIDTH) * jax.nn.silu(b_g)
    y_m = memory_attention(m_q, mem_n, m_wkv, m_qnorm, m_knorm) * jax.nn.silu(m_g)
    return x + jnp.concatenate([y_a, y_b, y_m], axis=-1) @ w_out

def odd_layer(x, mem_n, pos, norm_g, w_in, c_conv_w, c_conv_b, c_norm, d_qnorm, d_knorm,
              cmp_pos_k, cmp_w1_k, cmp_w2_k, cmp_pos_v, cmp_w1_v, cmp_w2_v,
              m_wkv, m_qnorm, m_knorm, w_out):
    Bz, S, _ = x.shape
    h = rms_norm(x, norm_g)
    c_a, c_b, c_g, d_q, d_kv, d_bg, d_g, m_q, m_g = split_cols(h @ w_in, ODD_SPLITS)
    y_c = conformer_conv(c_a, c_b, c_conv_w, c_conv_b, c_norm) * jax.nn.silu(c_g)
    kv = d_kv.reshape(Bz, S, 6, D_KV_GROUPS, HEAD_DIM)
    gates = jax.nn.sigmoid(d_bg.reshape(Bz, S, D_HEADS, 3))
    y_d = nsa(d_q.reshape(Bz, S, D_HEADS, HEAD_DIM), kv, gates, pos, d_qnorm, d_knorm,
              cmp_pos_k, cmp_w1_k, cmp_w2_k, cmp_pos_v, cmp_w1_v, cmp_w2_v) * jax.nn.silu(d_g)
    y_m = memory_attention(m_q, mem_n, m_wkv, m_qnorm, m_knorm) * jax.nn.silu(m_g)
    return x + jnp.concatenate([y_c, y_d, y_m], axis=-1) @ w_out

def first_inputs(seed: int = 0) -> dict:
    key = jax.random.key(seed)
    keys = iter(jax.random.split(key, 48))

    def nrm(shape, scale):
        return jax.random.normal(next(keys), shape, jnp.float32) * scale

    def gain(n):
        return 1.0 + nrm((n,), 0.05)

    return {
        "x": nrm((BATCH, SEQ, D_MODEL), 1.0),
        "mem": nrm((BATCH, MEM_TOKENS, D_MODEL), 1.0),
        "mem_norm": gain(D_MODEL),
        "l0_norm": gain(D_MODEL),
        "l0_w_in": nrm((D_MODEL, EVEN_IN), D_MODEL ** -0.5),
        "l0_a_vnorm": gain(A_WIDTH),
        "l0_a_ws": nrm((A_GROUPS, A_CHUNK, A_CHUNK), A_CHUNK ** -0.5),
        "l0_a_bs": 1.0 + nrm((A_GROUPS, A_CHUNK), 0.1),
        "l0_b_qnorm": gain(B_QK_DIM),
        "l0_b_knorm": gain(B_QK_DIM),
        "l0_b_lq1": nrm((B_QK_DIM,), 0.1),
        "l0_b_lk1": nrm((B_QK_DIM,), 0.1),
        "l0_b_lq2": nrm((B_QK_DIM,), 0.1),
        "l0_b_lk2": nrm((B_QK_DIM,), 0.1),
        "l0_b_subln": gain(B_V_DIM),
        "l0_m_wkv": nrm((D_MODEL, 2 * M_WIDTH), D_MODEL ** -0.5),
        "l0_m_qnorm": gain(HEAD_DIM),
        "l0_m_knorm": gain(HEAD_DIM),
        "l0_w_out": nrm((MIX_WIDTH, D_MODEL), MIX_WIDTH ** -0.5),
        "l1_norm": gain(D_MODEL),
        "l1_w_in": nrm((D_MODEL, ODD_IN), D_MODEL ** -0.5),
        "l1_c_conv_w": nrm((C_KERNEL, C_WIDTH), C_KERNEL ** -0.5),
        "l1_c_conv_b": nrm((C_WIDTH,), 0.02),
        "l1_c_norm": gain(C_WIDTH),
        "l1_d_qnorm": gain(HEAD_DIM),
        "l1_d_knorm": gain(HEAD_DIM),
        "l1_d_cmp_pos_k": nrm((CMP_BLOCK, HEAD_DIM), 0.02),
        "l1_d_cmp_w1_k": nrm((CMP_BLOCK * HEAD_DIM, CMP_HIDDEN), (CMP_BLOCK * HEAD_DIM) ** -0.5),
        "l1_d_cmp_w2_k": nrm((CMP_HIDDEN, HEAD_DIM), CMP_HIDDEN ** -0.5),
        "l1_d_cmp_pos_v": nrm((CMP_BLOCK, HEAD_DIM), 0.02),
        "l1_d_cmp_w1_v": nrm((CMP_BLOCK * HEAD_DIM, CMP_HIDDEN), (CMP_BLOCK * HEAD_DIM) ** -0.5),
        "l1_d_cmp_w2_v": nrm((CMP_HIDDEN, HEAD_DIM), CMP_HIDDEN ** -0.5),
        "l1_m_wkv": nrm((D_MODEL, 2 * M_WIDTH), D_MODEL ** -0.5),
        "l1_m_qnorm": gain(HEAD_DIM),
        "l1_m_knorm": gain(HEAD_DIM),
        "l1_w_out": nrm((MIX_WIDTH, D_MODEL), MIX_WIDTH ** -0.5),
    }

def first_block(x, mem, mem_norm,
              l0_norm, l0_w_in, l0_a_vnorm, l0_a_ws, l0_a_bs, l0_b_qnorm, l0_b_knorm,
              l0_b_lq1, l0_b_lk1, l0_b_lq2, l0_b_lk2, l0_b_subln, l0_m_wkv, l0_m_qnorm,
              l0_m_knorm, l0_w_out,
              l1_norm, l1_w_in, l1_c_conv_w, l1_c_conv_b, l1_c_norm, l1_d_qnorm, l1_d_knorm,
              l1_d_cmp_pos_k, l1_d_cmp_w1_k, l1_d_cmp_w2_k, l1_d_cmp_pos_v, l1_d_cmp_w1_v,
              l1_d_cmp_w2_v, l1_m_wkv, l1_m_qnorm, l1_m_knorm, l1_w_out):
    pos = jnp.arange(x.shape[1], dtype=jnp.int32)
    mem_n = rms_norm(mem, mem_norm)
    even_params = (l0_norm, l0_w_in, l0_a_vnorm, l0_a_ws, l0_a_bs, l0_b_qnorm, l0_b_knorm,
                   l0_b_lq1, l0_b_lk1, l0_b_lq2, l0_b_lk2, l0_b_subln, l0_m_wkv, l0_m_qnorm,
                   l0_m_knorm, l0_w_out)
    odd_params = (l1_norm, l1_w_in, l1_c_conv_w, l1_c_conv_b, l1_c_norm, l1_d_qnorm, l1_d_knorm,
                  l1_d_cmp_pos_k, l1_d_cmp_w1_k, l1_d_cmp_w2_k, l1_d_cmp_pos_v, l1_d_cmp_w1_v,
                  l1_d_cmp_w2_v, l1_m_wkv, l1_m_qnorm, l1_m_knorm, l1_w_out)
    for layer in range(DEPTH):
        if layer % 2 == 0:
            x = even_layer(x, mem_n, pos, layer + 1, *even_params)
        else:
            x = odd_layer(x, mem_n, pos, *odd_params)
    return x


DEPTH_2 = 1

CHUNK = 64
RET_HEADS = 4
RET_DK = 128
RET_DV = 256
RET_QK_WIDTH = RET_HEADS * RET_DK
RET_V_WIDTH = RET_HEADS * RET_DV
LRU_WIDTH = 1024
LRU_BLOCKS = 4
LRU_BLOCK = LRU_WIDTH // LRU_BLOCKS
LRU_CONV = 4
LRU_C = 8.0
LRU_MIN_RAD = 0.9
LRU_MAX_RAD = 0.999
D_FF = 3 * D_MODEL
FFN_CONV = 3
ROPE_BASE = 10000.0
RMS_EPS = 1e-6
GN_EPS = 1e-6

IN_SIZES = (RET_QK_WIDTH, RET_QK_WIDTH, RET_V_WIDTH, RET_V_WIDTH,
            LRU_WIDTH, LRU_WIDTH, D_MODEL, D_MODEL)
D_IN = sum(IN_SIZES)
SPLIT_POINTS = tuple(sum(IN_SIZES[:i + 1]) for i in range(len(IN_SIZES) - 1))


def rms_norm_2(x, w):
    x32 = x.astype(jnp.float32)
    y = x32 * lax.rsqrt(jnp.mean(x32 * x32, axis=-1, keepdims=True) + RMS_EPS)
    return (y * w.astype(jnp.float32)).astype(x.dtype)

def causal_depthwise_conv(x, w, b):
    k_width, channels = w.shape
    y = lax.conv_general_dilated(
        x, w[:, None, :].astype(x.dtype), window_strides=(1,),
        padding=[(k_width - 1, 0)], dimension_numbers=("NWC", "WIO", "NWC"),
        feature_group_count=channels)
    return y + b.astype(x.dtype)

def rotary(x, positions):
    half = x.shape[-1] // 2
    inv_freq = ROPE_BASE ** (-jnp.arange(half, dtype=jnp.float32) / half)
    ang = positions.astype(jnp.float32)[..., None] * inv_freq
    cos = jnp.cos(ang)[:, :, None, :]
    sin = jnp.sin(ang)[:, :, None, :]
    x32 = x.astype(jnp.float32)
    x1, x2 = x32[..., :half], x32[..., half:]
    return jnp.concatenate([x1 * cos - x2 * sin, x1 * sin + x2 * cos], axis=-1).astype(x.dtype)

def chunkwise_retention(q, k, v):
    bsz, seq, heads, dk = q.shape
    dv = v.shape[-1]
    n_chunks = seq // CHUNK
    log_gamma = jnp.log1p(-jnp.power(2.0, -5.0 - jnp.arange(heads, dtype=jnp.float32)))
    idx = jnp.arange(CHUNK, dtype=jnp.float32)
    dist = jnp.abs(idx[:, None] - idx[None, :])
    intra_decay = jnp.exp(log_gamma[:, None, None] * dist)
    q_decay = jnp.exp(log_gamma[:, None] * (idx + 1.0))
    k_decay = jnp.exp(log_gamma[:, None] * (CHUNK - 1.0 - idx))
    chunk_decay = jnp.exp(log_gamma * CHUNK)

    def to_chunks(t):
        return t.astype(jnp.float32).reshape(bsz, n_chunks, CHUNK, heads, -1).transpose(1, 0, 3, 2, 4)

    qc, kc, vc = to_chunks(q), to_chunks(k), to_chunks(v)

    def step(state, inp):
        qi, ki, vi = inp
        scores = jnp.einsum("bhid,bhjd->bhij", qi, ki) * intra_decay
        out = (jnp.einsum("bhij,bhjv->bhiv", scores, vi)
               + jnp.einsum("bhid,bhdv->bhiv", qi * q_decay[:, :, None], state))
        state = (state * chunk_decay[:, None, None]
                 + jnp.einsum("bhjd,bhjv->bhdv", ki * k_decay[:, :, None], vi))
        return state, out

    state0 = jnp.zeros((bsz, heads, dk, dv), jnp.float32)
    _, out = lax.scan(step, state0, (qc, kc, vc))
    return out.transpose(1, 0, 3, 2, 4).reshape(bsz, seq, heads, dv)

def head_group_norm(o, w):
    bsz, seq, heads, dv = o.shape
    mu = jnp.mean(o, axis=-1, keepdims=True)
    var = jnp.mean(jnp.square(o - mu), axis=-1, keepdims=True)
    y = (o - mu) * lax.rsqrt(var + GN_EPS)
    return y.reshape(bsz, seq, heads * dv) * w.astype(jnp.float32)

def _linear_recurrence_combine(e1, e2):
    a1, b1 = e1
    a2, b2 = e2
    return a1 * a2, a2 * b1 + b2

def rg_lru(x, w_r, b_r, w_i, b_i, lam):
    bsz, seq, width = x.shape
    x32 = x.astype(jnp.float32)
    xb = x32.reshape(bsz, seq, LRU_BLOCKS, LRU_BLOCK)
    r = jax.nn.sigmoid(jnp.einsum("bsni,nij->bsnj", xb, w_r.astype(jnp.float32))
                       + b_r.astype(jnp.float32)).reshape(bsz, seq, width)
    i = jax.nn.sigmoid(jnp.einsum("bsni,nij->bsnj", xb, w_i.astype(jnp.float32))
                       + b_i.astype(jnp.float32)).reshape(bsz, seq, width)
    log_a = -LRU_C * r * jax.nn.softplus(-lam.astype(jnp.float32))
    a = jnp.exp(log_a)
    b = jnp.sqrt(-jnp.expm1(2.0 * log_a)) * (i * x32)
    _, h = lax.associative_scan(_linear_recurrence_combine, (a, b), axis=1)
    return h

def second_inputs(seed: int = 0) -> dict:
    key = jax.random.key(seed)
    ks = jax.random.split(key, 24)

    def nrm(k, shape, scale):
        return jax.random.normal(k, shape, jnp.float32) * scale

    def gain(k, shape):
        return 1.0 + 0.02 * jax.random.normal(k, shape, jnp.float32)

    x = jax.random.normal(ks[0], (BATCH, SEQ, D_MODEL), jnp.float32)
    start = jax.random.randint(ks[1], (BATCH, 1), 0, 64) * CHUNK
    positions = (start + jnp.arange(SEQ)[None, :]).astype(jnp.int32)

    u = jax.random.uniform(ks[12], (DEPTH_2, LRU_WIDTH), jnp.float32,
                           LRU_MIN_RAD ** 2, LRU_MAX_RAD ** 2)
    a0 = jnp.sqrt(u)
    lru_lambda = jnp.log(a0) - jnp.log1p(-a0)

    return {
        "x": x,
        "positions": positions,
        "norm1_w": gain(ks[2], (DEPTH_2, D_MODEL)),
        "w_in": nrm(ks[3], (DEPTH_2, D_MODEL, D_IN), D_MODEL ** -0.5),
        "merge_gate_b": nrm(ks[4], (DEPTH_2, 2, D_MODEL), 0.02),
        "ret_gn_w": gain(ks[5], (DEPTH_2, RET_V_WIDTH)),
        "w_ret_o": nrm(ks[6], (DEPTH_2, RET_V_WIDTH, D_MODEL), RET_V_WIDTH ** -0.5),
        "lru_conv_w": nrm(ks[7], (DEPTH_2, LRU_CONV, LRU_WIDTH), LRU_CONV ** -0.5),
        "lru_conv_b": nrm(ks[8], (DEPTH_2, LRU_WIDTH), 0.02),
        "lru_w_r": nrm(ks[9], (DEPTH_2, LRU_BLOCKS, LRU_BLOCK, LRU_BLOCK), LRU_BLOCK ** -0.5),
        "lru_b_r": nrm(ks[10], (DEPTH_2, LRU_BLOCKS, LRU_BLOCK), 0.02),
        "lru_w_i": nrm(ks[11], (DEPTH_2, LRU_BLOCKS, LRU_BLOCK, LRU_BLOCK), LRU_BLOCK ** -0.5),
        "lru_b_i": nrm(ks[13], (DEPTH_2, LRU_BLOCKS, LRU_BLOCK), 0.02),
        "lru_lambda": lru_lambda,
        "w_lru_o": nrm(ks[14], (DEPTH_2, LRU_WIDTH, D_MODEL), LRU_WIDTH ** -0.5),
        "w_out": nrm(ks[15], (DEPTH_2, D_MODEL, D_MODEL), D_MODEL ** -0.5),
        "norm2_w": gain(ks[16], (DEPTH_2, D_MODEL)),
        "ffn_w_up": nrm(ks[17], (DEPTH_2, D_MODEL, 2 * D_FF), D_MODEL ** -0.5),
        "ffn_conv_w": nrm(ks[18], (DEPTH_2, FFN_CONV, D_FF), FFN_CONV ** -0.5),
        "ffn_conv_b": nrm(ks[19], (DEPTH_2, D_FF), 0.02),
        "ffn_w_down": nrm(ks[20], (DEPTH_2, D_FF, D_MODEL), D_FF ** -0.5),
        "norm_f_w": gain(ks[21], (D_MODEL,)),
    }

def second_block(x, positions, norm1_w, w_in, merge_gate_b, ret_gn_w, w_ret_o,
              lru_conv_w, lru_conv_b, lru_w_r, lru_b_r, lru_w_i, lru_b_i, lru_lambda,
              w_lru_o, w_out, norm2_w, ffn_w_up, ffn_conv_w, ffn_conv_b, ffn_w_down,
              norm_f_w):
    bsz, seq, _ = x.shape
    for l in range(DEPTH_2):
        h = rms_norm_2(x, norm1_w[l])
        proj = h @ w_in[l]
        q, k, v, g_ret, x_lru, y_lru, gate_ret, gate_lru = jnp.split(proj, SPLIT_POINTS, axis=-1)

        q = rotary(q.reshape(bsz, seq, RET_HEADS, RET_DK), positions)
        k = rotary(k.reshape(bsz, seq, RET_HEADS, RET_DK), positions) * (RET_DK ** -0.5)
        o = chunkwise_retention(q, k, v.reshape(bsz, seq, RET_HEADS, RET_DV))
        o = head_group_norm(o, ret_gn_w[l])
        y_a = (o * jax.nn.silu(g_ret.astype(jnp.float32))).astype(x.dtype) @ w_ret_o[l]

        xc = causal_depthwise_conv(x_lru, lru_conv_w[l], lru_conv_b[l])
        hl = rg_lru(xc, lru_w_r[l], lru_b_r[l], lru_w_i[l], lru_b_i[l], lru_lambda[l])
        y_b = (hl * jax.nn.gelu(y_lru.astype(jnp.float32))).astype(x.dtype) @ w_lru_o[l]

        mix = (jax.nn.sigmoid(gate_ret + merge_gate_b[l, 0]) * y_a
               + jax.nn.sigmoid(gate_lru + merge_gate_b[l, 1]) * y_b)
        x = x + mix @ w_out[l]

        h = rms_norm_2(x, norm2_w[l])
        up = h @ ffn_w_up[l]
        gate, val = jnp.split(up, [D_FF], axis=-1)
        gate = causal_depthwise_conv(gate, ffn_conv_w[l], ffn_conv_b[l])
        x = x + (jax.nn.gelu(gate) * val) @ ffn_w_down[l]
    return rms_norm_2(x, norm_f_w)


def setup_inputs(seed=0):
    out = dict(first_inputs(seed))
    for name, value in second_inputs(seed + 1).items():
        if name != "x":
            out[name + "_2"] = value
    return out


def reference(
    x, mem, mem_norm, l0_norm, l0_w_in, l0_a_vnorm, l0_a_ws, l0_a_bs, l0_b_qnorm, l0_b_knorm,
    l0_b_lq1, l0_b_lk1, l0_b_lq2, l0_b_lk2, l0_b_subln, l0_m_wkv, l0_m_qnorm, l0_m_knorm,
    l0_w_out, l1_norm, l1_w_in, l1_c_conv_w, l1_c_conv_b, l1_c_norm, l1_d_qnorm, l1_d_knorm,
    l1_d_cmp_pos_k, l1_d_cmp_w1_k, l1_d_cmp_w2_k, l1_d_cmp_pos_v, l1_d_cmp_w1_v, l1_d_cmp_w2_v,
    l1_m_wkv, l1_m_qnorm, l1_m_knorm, l1_w_out, positions_2, norm1_w_2, w_in_2, merge_gate_b_2,
    ret_gn_w_2, w_ret_o_2, lru_conv_w_2, lru_conv_b_2, lru_w_r_2, lru_b_r_2, lru_w_i_2,
    lru_b_i_2, lru_lambda_2, w_lru_o_2, w_out_2, norm2_w_2, ffn_w_up_2, ffn_conv_w_2,
    ffn_conv_b_2, ffn_w_down_2, norm_f_w_2,
):
    x = first_block(
        x, mem, mem_norm, l0_norm, l0_w_in, l0_a_vnorm, l0_a_ws, l0_a_bs, l0_b_qnorm,
        l0_b_knorm, l0_b_lq1, l0_b_lk1, l0_b_lq2, l0_b_lk2, l0_b_subln, l0_m_wkv, l0_m_qnorm,
        l0_m_knorm, l0_w_out, l1_norm, l1_w_in, l1_c_conv_w, l1_c_conv_b, l1_c_norm, l1_d_qnorm,
        l1_d_knorm, l1_d_cmp_pos_k, l1_d_cmp_w1_k, l1_d_cmp_w2_k, l1_d_cmp_pos_v, l1_d_cmp_w1_v,
        l1_d_cmp_w2_v, l1_m_wkv, l1_m_qnorm, l1_m_knorm, l1_w_out,
    )
    return second_block(
        x, positions_2, norm1_w_2, w_in_2, merge_gate_b_2, ret_gn_w_2, w_ret_o_2, lru_conv_w_2,
        lru_conv_b_2, lru_w_r_2, lru_b_r_2, lru_w_i_2, lru_b_i_2, lru_lambda_2, w_lru_o_2,
        w_out_2, norm2_w_2, ffn_w_up_2, ffn_conv_w_2, ffn_conv_b_2, ffn_w_down_2, norm_f_w_2,
    )


_drawn_inputs = setup_inputs


def setup_inputs(seed=0):
    import zlib

    import numpy as np

    out = dict(_drawn_inputs(seed))
    spreads = {}
    factors = {'mem_norm': 8.0,
     'l0_a_vnorm': 5.371,
     'l0_b_qnorm': 3.176,
     'l0_b_knorm': 3.023,
     'l0_b_lk1': 3.407,
     'l0_b_lq2': 200.0,
     'l0_b_subln': 3.843,
     'l0_m_qnorm': 8.0,
     'l0_m_knorm': 8.0,
     'l1_c_conv_b': 4.896,
     'l1_c_norm': 3.642,
     'l1_d_qnorm': 8.0,
     'l1_d_knorm': 8.0,
     'l1_d_cmp_pos_k': 21.539,
     'l1_d_cmp_pos_v': 31.072,
     'l1_m_qnorm': 8.0,
     'l1_m_knorm': 8.0,
     'norm1_w_2': 4.024,
     'merge_gate_b_2': 8.0,
     'ret_gn_w_2': 21.809,
     'lru_conv_b_2': 20.762,
     'lru_b_r_2': 49.715,
     'lru_b_i_2': 41.483,
     'norm2_w_2': 13.13,
     'ffn_conv_b_2': 19.313,
     'norm_f_w_2': 22.813}
    for name, (base, spread) in spreads.items():
        noise = np.random.default_rng([zlib.crc32(name.encode()), seed]).standard_normal(out[name].shape)
        drawn = base * np.exp(spread * noise) if base else spread * noise
        out[name] = __import__('jax').numpy.asarray(drawn.astype(out[name].dtype))
    for name, factor in factors.items():
        out[name] = (out[name] * factor).astype(out[name].dtype)
    return out
```

```python
from contextlib import ExitStack

import numpy as np

import concourse.bass as bass
from concourse import mybir

F32 = mybir.dt.float32
I32 = mybir.dt.int32
ALU = mybir.AluOpType
ACT = mybir.ActivationFunctionType
AX_X = mybir.AxisListType.X

P = 128
S = 256
T = S // P
D = 1024
KT = D // P
CH = 512
BLK = KT * CH
SLOTS = 5
EPS = 1e-6
FAR = 1e30
GELU_C = 0.7978845608028654
GELU_A = 0.044715
LAM_INIT = 0.8 - 0.6 * float(np.exp(-0.3))
TWO_PI_PARTS = (6.28125, 4059 / 2 ** 21, 2 * np.pi - 6.28125 - 4059 / 2 ** 21)
PI_BELOW = 3.1415925
ROUND = 1.5 * 2 ** 23
N_CMP = 15
RET_HEADS = 4
FFN_STEPS = 6

EARLY = [("ident", P), ("causal", 3 * P), ("tril_t", P), ("cos0", 2 * 4), ("sin0", 2 * 4),
         ("mem_norm", KT), ("l0_norm", KT), ("a_vnorm", 512), ("a_bs", 4), ("a_ws_t", 512),
         ("b_qnorm", 32), ("b_knorm", 32), ("b_lq1", 32), ("b_lk1", 32), ("b_lq2", 32), ("b_lk2", 32),
         ("b_subln", 64), ("m0_qnorm", 64), ("m0_knorm", 64), ("m1_qnorm", 64), ("m1_knorm", 64),
         ("l1_norm", KT), ("cos1", 2 * 8), ("sin1", 2 * 8), ("cos_cmp", 8), ("sin_cmp", 8),
         ("cmp_mask", 2 * 16), ("cmp_valid", 2), ("conv_w", 4 * 31), ("conv_b", 4), ("c_norm", 512),
         ("d_qnorm", 64), ("d_knorm", 64), ("cmp_pos", 32), ("cmp_w2", 128), ("inv_freq", 64)]
LATE = [("norm1", KT), ("decay", RET_HEADS * 3 * P), ("ret_gn", KT), ("merge_b", 2 * KT), ("lru_conv_w", KT * 4),
        ("lru_conv_b", KT), ("lru_b_r", KT), ("lru_b_i", KT), ("lru_lambda", KT), ("norm2", KT),
        ("ffn_conv_w", 24 * 3), ("ffn_conv_b", 24), ("norm_f", D)]


def offsets(spec):
    out, at = {}, 0
    for name, width in spec:
        out[name] = (at, width)
        at += width
    return out, at


L0_FILL = ["a_v", "a_u", "a_g", "b_g"]
L1_FILL = ["c_b", "c_a", "c_g", "d_g"]
BLOCKS = [("kv0", 1), ("kv1", 1), ("b_q", 1), ("b_k", 1), ("m_qg0", 1), ("b_v", 1),
          ("a_v", 1), ("a_u", 1), ("a_g", 1), ("b_g", 1), ("out0_r", 3), ("out0_a", 1), ("out0_b", 3),
          ("d_q", 1), ("dkv1", 1), ("dkv2", 1), ("cmp_w1", 1), ("m_qg1", 1),
          ("c_b", 1), ("c_a", 1), ("c_g", 1), ("d_g", 1), ("out1_r", 3), ("out1_a", 1), ("out1_b", 3)]
BLOCKS += [(b, 1) for b in ["x_lru0", "x_lru1", "r_q", "r_k", "y_lru0", "y_lru1", "lru_w", "r_v0", "r_v1", "g_ret0",
                            "g_ret1"] + [f"{n}{b}" for b in range(2) for n in ("gate_r", "gate_l", "ret_o", "lru_o")]
           + ["mix_out0", "mix_out1"] + [f"{n}{i}" for i in range(FFN_STEPS) for n in ("up_g", "up_v", "down")]]


MIX_ORDER = [f"{n}{b}" for b in range(2) for n in ("gate_r", "gate_l", "ret_o", "lru_o")]


class Ring:

    def __init__(self, full, free, names):
        self.full, self.free, self.names = full, free, names
        self.index = {n: i for i, n in enumerate(names)}
        assert len(self.index) == len(names)

    def slot(self, name):
        return self.index[name] % len(self.full)

    def claim(self, eng, name):
        turn = self.index[name] // len(self.full)
        if turn > 0:
            eng.wait_ge(self.free[self.slot(name)], turn)

    def arrived(self, eng, name):
        eng.wait_ge(self.full[self.slot(name)], self.index[name] // len(self.full) + 1)

    def read(self, eng, name):
        eng.wait_ge(self.free[self.slot(name)], self.index[name] // len(self.full) + 1)

    def filled(self, ins, name):
        ins.then_inc(self.full[self.slot(name)], 1)

    def freed(self, ins, name, eng):
        ins.then_inc(self.free[self.slot(name)], 1)
        self.read(eng, name)


class Milestones:

    def __init__(self, sem, names):
        self.sem, self.names, self.done = sem, names, 0

    def mark(self, ins, name, eng):
        assert self.names[self.done] == name, (self.names[self.done], name)
        self.done += 1
        ins.then_inc(self.sem, 1)
        eng.wait_ge(self.sem, self.done)

    def wait(self, eng, name):
        eng.wait_ge(self.sem, self.names.index(name) + 1)


class Chain:

    def __init__(self, eng, sem):
        self.eng, self.sem, self.count = eng, sem, 0

    def __call__(self, ins):
        self.count += 1
        ins.then_inc(self.sem, 1)
        self.eng.wait_ge(self.sem, self.count)


class Unit:
    def __init__(self, kind, head, sub=0):
        self.kind, self.head, self.sub = kind, head, sub
        self.causal = kind in ("diff", "slc", "win")
        self.k_rows = 32 if kind == "diff" else 64
        self.scale = float(self.k_rows) ** -0.5
        if kind == "cmp":
            self.keys, self.blocks = (16, 16), [(0, 0), (1, 0)]
        elif self.causal:
            self.keys, self.blocks = (P, S), [(0, 0), (1, 0), (1, 1)]
        else:
            self.keys, self.blocks = (S, S), [(0, 0), (0, 1), (1, 0), (1, 1)]
        self.width = sum(self.keys)

    def seg(self, t):
        return slice(self.keys[0] * t, self.keys[0] * t + self.keys[t])

    def cols(self, t, kb):
        at = self.keys[0] * t + P * kb
        return slice(at, at + min(P, self.keys[t]))


UNITS0 = [Unit("mem", h) for h in range(4)] + [Unit("diff", h, m) for h in range(8) for m in range(2)]
UNITS1 = [Unit("mem", h) for h in range(4)] + [Unit(k, h) for h in range(8) for k in ("cmp", "slc", "win")]
FILL_MM = 4 * T * KT


def fill_after(i, n):
    return min(FILL_MM, FILL_MM * (i + 1) // n)


def pieces_at(i, n):
    before = fill_after(i - 1, n) // KT if i else 0
    return range(before, fill_after(i, n) // KT)


def xpose_names():
    out = [f"mem{j}" for j in range(4)] + [f"x0_{j}" for j in range(4)]
    out += ["mk0", "mk1", "q0", "q1", "k0", "k1", "mq0"]
    out += [("unit", i) for i in range(len(UNITS0))]
    out += ["z0", "z1", "ym0", "ya0_0", "ya0_1", "yb0_0", "yb0_1"]
    out += [f"x1_{j}" for j in range(4)] + ["cmp", "dq0", "dq1", "hid_k", "hid_v", "dk0", "dk1", "kvc", "kc", "mq1"]
    out += [("unit", len(UNITS0) + i) for i in range(len(UNITS1))]
    out += ["yc0", "yc1", "ym1", "yb1_0", "yb1_1", "ya1_0", "ya1_1"]
    out += [f"x2_{j}" for j in range(4)] + ["rq0", "rq1", "rk0", "rk1"] + [("ret", h) for h in range(RET_HEADS)]
    out += [f"ret_y{j}" for j in range(4)] + [f"x3_{j}" for j in range(4)]
    return out


def proj_names():
    rows = lambda b: [(b, t) for t in range(T)]
    out = []
    for b in ["kv0", "kv1", "b_q", "b_k", "m_qg0", "b_v"] + L0_FILL + ["out0_a", "out0_b"] + \
            ["d_q", "dkv1", "dkv2", "m_qg1"] + L1_FILL + ["out1_a", "out1_b"] + \
            ["x_lru0", "x_lru1", "r_q", "r_k", "y_lru0", "y_lru1"]:
        out += rows(b)
    out += [(f"lru_{n}", b) for b in range(4) for n in "ri"]
    for b in ["r_v0", "r_v1", "g_ret0", "g_ret1"] + MIX_ORDER + ["mix_out0", "mix_out1"]:
        out += rows(b)
    for i in range(FFN_STEPS):
        out += rows(f"up_g{i}") + rows(f"up_v{i}")
    return out




def build(nc, early_d, late_d, positions_d, x_d, mem_d, blocks_d, out_d):
    e_at, e_width = offsets(EARLY)
    l_at, l_width = offsets(LATE)
    block_index = {b: i for i, (b, _) in enumerate(BLOCKS)}
    with ExitStack() as ctx:
        def sb(name, shape, dt=F32):
            return ctx.enter_context(nc.sbuf_tensor(name, shape, dt))

        def sem(name):
            return ctx.enter_context(nc.semaphore(name))

        x = sb("x", [P, T, D])
        h_rows = sb("h_rows", [P, T, D])
        rows = sb("rows", [P, T, 4096])
        h_t = sb("h_t", [P, KT, S])
        y_t = sb("y_t", [P, 10, S])
        weights = sb("weights", [P, SLOTS, BLK])
        early = sb("early", [P, e_width])
        attention = sb("attention", [P, 3584])
        mkv = attention[:, 0:2048].rearrange("p (l t n) -> p l t n", l=2, t=T)
        mk_t = attention[:, 2048:3072].rearrange("p (l a s) -> p l a s", l=2, a=2)
        mq_t = attention[:, 3072:3584].rearrange("p (a s) -> p a s", a=2)
        late = attention[:, 0:l_width]
        positions = sb("positions", [P, T], I32)
        cos2 = sb("cos2", [P, T * 64])
        sin2 = sb("sin2", [P, T * 64])
        half_bias = sb("half_bias", [P, 4 * KT])
        decay_coef = sb("decay_coef", [P, 2, KT])
        lam_exp_in = sb("lam_exp_in", [P, KT])
        head_sums = sb("head_sums", [P, T, RET_HEADS])
        q_t = sb("q_t", [P, 4, S])
        k_t = sb("k_t", [P, 4, S])
        logits = sb("logits", [P, 3, 512])
        gate_tmp = logits[:, 2, :].rearrange("p (t n) -> p t n", t=T)
        probs_t = sb("probs_t", [P, 2, 512])
        scratch = sb("scratch", [P, 1024])
        rope_tmp = sb("rope_tmp", [P, 4, P])
        ws_masked = sb("ws_masked", [P, 512])
        sumsq = sb("sumsq", [P, 64])
        x_sums = sb("x_sums", [P, 6, T])
        coef = sb("coef", [P, T])
        mean_sq = sb("mean_sq", [P, 2, 64])
        rstd = sb("rstd", [P, 2, 64])
        minus_half = sb("minus_half", [P, 64])
        neg_max = sb("neg_max", [P, 2, T])
        row_sum = sb("row_sum", [P, 2, T])
        row_inv = sb("row_inv", [P, T])
        row_scale = sb("row_scale", [P, T])
        lam_tmp = sb("lam_tmp", [P, 8])

        gates = sb("gates", [P, T, 24])
        conv_in = y_t[:, 0:5, :].rearrange("p k s -> p (k s)")[:, 0:4 * (S + 30)].rearrange("p (f s) -> p f s", f=4)
        conv_out = h_rows[:, 0, :].rearrange("p (f s) -> p f s", s=S)
        cmp_blocks = h_rows[:, 1, 0:64 * N_CMP].rearrange("p (a g n j) -> p a g n j", a=2, g=2, j=16)
        hid_tmp = sb("hid_tmp", [P, 2, 30])
        hid = sb("hid", [P, 2, 30])
        kvc = sb("kvc", [P, 2, 2, 64])
        kc_rows = logits[:, 1, 0:256].rearrange("p (g c d) -> p g c d", g=2, d=64)
        kc_t = sb("kc_t", [P, 2, 16])
        act_tmp = sb("act_tmp", [P, 2, 512])

        psum = ctx.enter_context(nc.psum_tensor("psum", [P, 8, 512], F32))
        PROJ_BANK, SCORE_BANK, XPOSE_BANK, OUT_BANK = 0, 2, 4, 6

        def E(name, rows_=P):
            at, width = e_at[name]
            return early[0:rows_, at:at + width]

        def L(name):
            at, width = l_at[name]
            return late[:, at:at + width]

        def tile_of(c0, f):
            return rows[:, f // 4, c0 + S * (f % 4):c0 + S * (f % 4 + 1)]

        def pair_of(c0, i):
            return rows[:, i // 2, c0 + 512 * (i % 2):c0 + 512 * (i % 2 + 1)]

        ident = E("ident")

        loaded = {n: sem(f"{n}_loaded") for n in ("early", "mem", "x", "positions", "late")}
        block_landed = [sem(f"block_landed{i}") for i in range(SLOTS)]
        proj = Ring([sem(f"proj_full{i}") for i in range(2)], [sem(f"proj_free{i}") for i in range(2)], proj_names())
        xpose = Ring([sem(f"xpose_full{i}") for i in range(2)], [sem(f"xpose_free{i}") for i in range(2)],
                     xpose_names())
        n_units = len(UNITS0) + len(UNITS1)
        score = Ring([sem(f"score_full{i}") for i in range(2)], [sem(f"score_free{i}") for i in range(2)],
                     list(range(n_units + RET_HEADS)))
        logits_ready = sem("logits_ready")
        exp_done = sem("exp_done")
        probs_ready = sem("probs_ready")
        pv_done = sem("pv_done")
        heads_out = Milestones(sem("heads_out"), ["mem0", "diff", "mem1", "nsa"])
        normed = Milestones(sem("normed"), ["mem", "x0", "mk0", "mk1", "q", "k", "mq0", "a_v", "y_m0", "y_a0", "y_b",
                                               "x1", "dq", "dk", "cmp_blocks", "hid", "kc", "mq1", "conv", "y_m1",
                                               "y_d", "y_c", "x2", "xc", "rq", "rk", "lru_y", "g_ret", "mix", "x3"])
        NORMS = [("mem", 2), ("x0", 2), ("mk0", 8), ("mk1", 8), ("q", 32), ("k", 32), ("mq0", 8), ("a_v", 8),
                 ("y_b", 16), ("x1", 2), ("dq", 16), ("dk", 8), ("kc", 2), ("mq1", 8), ("y_c", 2), ("x2", 2), ("gn0", 4), ("gn1", 4),
                 ("x3", 2), ("final", 2)]
        mean_ready = Milestones(sem("mean_ready"), [n for n, _ in NORMS])
        rstd_ready = Milestones(sem("rstd_ready"), [n for n, _ in NORMS])
        squares = Milestones(sem("squares"), ["mem", "x0", "x1", "x2", "x3", "final"])
        lam_dots = sem("lam_dots")
        lam_exp = sem("lam_exp")
        gate_m = Milestones(sem("gate_m"), [0, 1])
        fill_act = Milestones(sem("fill_act"), [(0, k, p) for p in range(8) for k in (("square", "tanh") if p < 4 else ("tanh",))] +
                              [(1, "tanh", p) for p in range(4, 8)])
        fill_poly = Milestones(sem("fill_poly"), [(0, p) for p in range(4)])
        ws_ready = sem("ws_ready")
        x_ready = Milestones(sem("x_ready"), ["x1", "x2", "x3", "final"])
        gates_tanh = sem("gates_tanh")
        hid_tanh = Milestones(sem("hid_tanh"), ["k", "v"])
        yc_tanh = sem("yc_tanh")
        yc_normed = sem("yc_normed")
        sin_args, sin_ready = sem("sin_args"), sem("sin_ready")
        lru_coef = sem("lru_coef")
        lam_neg, lam_neg_exp = sem("lam_neg"), sem("lam_neg_exp")
        lru_in = sem("lru_in")
        lru_exp = sem("lru_exp")
        lru_ratio, lru_root = sem("lru_ratio"), sem("lru_root")
        y_lru_ready = sem("y_lru_ready")
        ret_sums = sem("ret_sums")
        ret_decayed = sem("ret_decayed")
        g_tanh = sem("g_tanh")
        mix_tanh = sem("mix_tanh")
        conv_gate, conv_gelu, ffn_ready = sem("conv_gate"), sem("conv_gelu"), sem("ffn_ready")
        down_done, down_read = sem("down_done"), sem("down_read")
        out_ready = sem("out_ready")
        vec_chain, act_chain, pool_chain = sem("vec_chain"), sem("act_chain"), sem("pool_chain")
        stored = sem("stored")

        def wait_block(eng, block):
            i = block_index[block]
            eng.wait_ge(block_landed[i % SLOTS], 16 * (i // SLOTS + 1))

        def turned(eng, *names):
            for name in names:
                xpose.read(eng, name)

        def chunk_read(eng, name):
            for t in range(T):
                proj.read(eng, (name, t))

        def block_view(block, cols=CH):
            return weights[:, block_index[block] % SLOTS, :].rearrange("p (k n) -> p k n", n=cols)

        last_use = {b: (b, 1) for b, _ in BLOCKS}
        last_use.update({"out0_r": ("out0_b", 1), "out1_r": ("out1_b", 1), "cmp_w1": "hid_v",
                         "lru_w": ("lru_i", 3), **{f"down{i}": ("down", i) for i in range(FFN_STEPS)}})

        block_ = ctx.enter_context(nc.Block())

        @block_.sync
        def _(sp):
            sp.dma_start(rows[:, :, 0:D], mem_d.rearrange("(t p) d -> p t d", p=P)).then_inc(loaded["mem"], 16)
            sp.dma_start(early[:, :], early_d).then_inc(loaded["early"], 16)
            sp.dma_start(x[:, :, :], x_d.rearrange("(t p) d -> p t d", p=P)).then_inc(loaded["x"], 16)
            sp.dma_start(positions[:, :], positions_d).then_inc(loaded["positions"], 16)
            for i, (name, kind) in enumerate(BLOCKS):
                if i >= SLOTS:
                    user = last_use[BLOCKS[i - SLOTS][0]]
                    if user[0] == "down":
                        sp.wait_ge(down_done, user[1] + 1)
                    else:
                        (xpose if user == "hid_v" else proj).arrived(sp, user)
                sp.dma_start(weights[:, i % SLOTS, :], blocks_d[i]).then_inc(block_landed[i % SLOTS], 16)
            sp.wait_ge(out_ready, 1)
            sp.dma_start(out_d.rearrange("(t p) d -> p t d", p=P), h_rows[:, :, :]).then_inc(stored, 16)
            sp.wait_ge(stored, 16)

        @block_.gpsimd
        def _(pool):
            link = Chain(pool, pool_chain)
            link(nc.gpsimd.memset(minus_half[:, :], -0.5))
            for n, (name, width) in enumerate(NORMS):
                mean_ready.wait(pool, name)
                rstd_ready.mark(nc.gpsimd.tensor_tensor(rstd[:, n % 2, 0:width], mean_sq[:, n % 2, 0:width],
                                                        minus_half[:, 0:width], ALU.pow), name, pool)

        @block_.tensor
        def _(pe):
            def rows_piece(name, t, src, cols=CH):
                proj.claim(pe, (name, t))
                wait_block(pe, name)
                w = block_view(name)
                for k in range(KT):
                    mm = nc.tensor.matmul(psum[:, PROJ_BANK + proj.slot((name, t)), 0:cols],
                                          src[:, k, t * P:(t + 1) * P], w[:, k, 0:cols],
                                          start=(k == 0), stop=(k == KT - 1))
                    if k == KT - 1:
                        proj.filled(mm, (name, t))
                    yield

            def features_piece(name, half, src):
                proj.claim(pe, (name, half))
                wait_block(pe, name)
                w = block_view(name)
                for a in range(2):
                    for k in range(KT):
                        mm = nc.tensor.matmul(psum[:, PROJ_BANK + proj.slot((name, half)), a * S:(a + 1) * S],
                                              w[:, k, (2 * half + a) * P:(2 * half + a + 1) * P], src[:, k, :],
                                              start=(k == 0), stop=(k == KT - 1))
                        if a == 1 and k == KT - 1:
                            proj.filled(mm, (name, half))
                        if k % 2 == 1:
                            yield

            def project(name, src, cols=CH):
                for t in range(T):
                    for _ in rows_piece(name, t, src, cols):
                        pass

            def turn_pair(name, tiles):
                xpose.claim(pe, name)
                bank = psum[:, XPOSE_BANK + xpose.slot(name), :]
                for j in range(2):
                    for t in range(T):
                        at = j * S + t * P
                        mm = nc.tensor.transpose(bank[:, at:at + P], tiles(j, t), ident)
                xpose.filled(mm, name)

            def unit_scores(i, u, q, k):
                score.claim(pe, i)
                for t in range(T):
                    mm = nc.tensor.matmul(psum[:, SCORE_BANK + score.slot(i), u.seg(t)],
                                          q[:, t * P:(t + 1) * P], k[:, 0:u.keys[t]], start=True, stop=True)
                score.filled(mm, i)

            def unit_turn(i, u):
                pe.wait_ge(probs_ready, i + 1)
                xpose.claim(pe, ("unit", i))
                bank = psum[:, XPOSE_BANK + xpose.slot(("unit", i)), :]
                for n, (t, kb) in enumerate(u.blocks):
                    rows_ = u.cols(t, kb).stop - u.cols(t, kb).start
                    mm = nc.tensor.transpose(bank[0:rows_, n * P:(n + 1) * P], logits[:, i % 3, u.cols(t, kb)], ident)
                xpose.filled(mm, ("unit", i))

            def unit_values(i, u, v, col, first, last):
                xpose.read(pe, ("unit", i))
                for n, (t, kb) in enumerate(u.blocks):
                    ends = n + 1 == len(u.blocks) or u.blocks[n + 1][0] != t
                    mm = nc.tensor.matmul(psum[:, OUT_BANK + t, col:col + 64],
                                          probs_t[0:v(kb).shape[0], i % 2, n * P:(n + 1) * P],
                                          v(kb), start=(first and kb == 0), stop=(last and ends),
                                          skip_group_check=True)
                mm.then_inc(pv_done, 1)

            pe.wait_ge(loaded["early"], 16)
            normed.wait(pe, "mem")
            for j in range(4):
                turn_pair(f"mem{j}", lambda a, t: rows[:, t, (2 * j + a) * P:(2 * j + a + 1) * P])
            turned(pe, "mem2", "mem3")
            project("kv0", y_t)
            project("kv1", y_t)
            normed.wait(pe, "x0")
            for j in range(4):
                turn_pair(f"x0_{j}", lambda a, t: h_rows[:, t, (2 * j + a) * P:(2 * j + a + 1) * P])
            turned(pe, "x0_2", "x0_3")
            project("b_q", h_t)
            for l in range(2):
                normed.wait(pe, f"mk{l}")
                turn_pair(f"mk{l}", lambda a, t: mkv[:, l, t, a * P:(a + 1) * P])
            project("b_k", h_t)
            normed.wait(pe, "q")
            for j in range(2):
                turn_pair(f"q{j}", lambda a, t: rows[:, t, 1536 + (2 * j + a) * P:1536 + (2 * j + a + 1) * P])
            project("m_qg0", h_t)
            normed.wait(pe, "k")
            for j in range(2):
                turn_pair(f"k{j}", lambda a, t: rows[:, t, 2048 + (2 * j + a) * P:2048 + (2 * j + a + 1) * P])
            project("b_v", h_t)
            normed.wait(pe, "mq0")
            turn_pair("mq0", lambda a, t: rows[:, t, 3584 + a * P:3584 + (a + 1) * P])
            turned(pe, "k0", "k1", "mq0")
            turned(pe, "q0", "q1", "mk0", "mk1")
            chunk_read(pe, "b_v")
            chunk_read(pe, "kv0")

            def operands0(u):
                if u.kind == "mem":
                    r, j = 64 * (u.head % 2), u.head // 2
                    return (mq_t[r:r + 64, j, :], mk_t[r:r + 64, 0, j, :],
                            lambda kb: mkv[:, 0, kb, 256 + 64 * u.head:320 + 64 * u.head], 64 * u.head, True, True)
                r, j = 32 * ((2 * u.head + u.sub) % 4), u.head // 2
                return (q_t[r:r + 32, j, :], k_t[r:r + 32, j, :],
                        lambda kb: rows[:, kb, 2560 + 64 * u.head:2624 + 64 * u.head], 64 * u.head,
                        u.sub == 0, u.sub == 1)

            def layer_units(units, base, operands, fill, group_starts):
                filler = (s for name in fill for t in range(T)
                          for s in (features_piece if name in ("c_a", "c_b") else rows_piece)(name, t, h_t))
                n = len(units)
                issued = 0
                for i in range(n + 2):
                    if i < n:
                        unit_scores(base + i, units[i], *operands(units[i])[0:2])
                    while issued < fill_after(i, n):
                        next(filler, None)
                        issued += 1
                    if 1 <= i <= n:
                        unit_turn(base + i - 1, units[i - 1])
                    if i >= 2:
                        if i - 2 in group_starts:
                            heads_out.wait(pe, group_starts[i - 2])
                        unit_values(base + i - 2, units[i - 2], *operands(units[i - 2])[2:])
                for _ in filler:
                    pass

            layer_units(UNITS0, 0, operands0, L0_FILL, {4: "mem0"})
            pe.wait_ge(ws_ready, 1)
            normed.wait(pe, "a_v")
            for t in range(T):
                xpose.claim(pe, f"z{t}")
                for g in range(4):
                    mm = nc.tensor.matmul(psum[:, XPOSE_BANK + xpose.slot(f"z{t}"), g * P:(g + 1) * P],
                                          ws_masked[:, g * P:(g + 1) * P], rows[:, t, 512 + g * P:512 + (g + 1) * P],
                                          start=True, stop=True)
                xpose.filled(mm, f"z{t}")
            normed.wait(pe, "y_m0")
            turn_pair("ym0", lambda a, t: rows[:, t, 3840 + a * P:3840 + (a + 1) * P])
            normed.wait(pe, "y_a0")
            for j in range(2):
                turn_pair(f"ya0_{j}", lambda a, t: rows[:, t, (2 * j + a) * P:(2 * j + a + 1) * P])
            normed.wait(pe, "y_b")
            for j in range(2):
                turn_pair(f"yb0_{j}", lambda a, t: rows[:, t, 3072 + (2 * j + a) * P:3072 + (2 * j + a + 1) * P])

            def out_project(layer):
                rest = block_view(f"out{layer}_r", 1024)
                for half, name in enumerate((f"out{layer}_a", f"out{layer}_b")):
                    wait_block(pe, f"out{layer}_r")
                    wait_block(pe, name)
                    w = block_view(name)
                    for t in range(T):
                        proj.claim(pe, (name, t))
                        for n, k in enumerate([8, 9] + list(range(8))):
                            if half == 0 and t == 0 and k in (8, 0, 4):
                                turned(pe, *{8: [f"ym{layer}"], 0: [f"ya{layer}_{j}" for j in range(2)],
                                             4: [f"yb{layer}_{j}" for j in range(2)]}[k])
                            rhs = rest[:, k - 8, half * CH:(half + 1) * CH] if k >= 8 else w[:, k, :]
                            mm = nc.tensor.matmul(psum[:, PROJ_BANK + proj.slot((name, t)), :],
                                                  y_t[:, k, t * P:(t + 1) * P], rhs, start=(n == 0), stop=(n == 9))
                        proj.filled(mm, (name, t))

            out_project(0)

            normed.wait(pe, "x1")
            for j in range(4):
                turn_pair(f"x1_{j}", lambda a, t: h_rows[:, t, (2 * j + a) * P:(2 * j + a + 1) * P])
            turned(pe, "x1_2", "x1_3")
            project("d_q", h_t)
            project("dkv1", h_t)
            chunk_read(pe, "dkv1")
            turn_pair("cmp", lambda a, t: rows[:, t, 512 + a * P:512 + (a + 1) * P])
            normed.wait(pe, "dq")
            for j in range(2):
                turn_pair(f"dq{j}", lambda a, t: rows[:, t, (2 * j + a) * P:(2 * j + a + 1) * P])
            project("dkv2", h_t, 280)
            normed.wait(pe, "cmp_blocks")
            wait_block(pe, "cmp_w1")
            w1 = weights[:, block_index["cmp_w1"] % SLOTS, :].rearrange("p (j h) -> p j h", h=P)
            for r, name in ((0, "hid_k"), (64, "hid_v")):
                xpose.claim(pe, name)
                for j in range(32):
                    mm = nc.tensor.matmul(psum[:, XPOSE_BANK + xpose.slot(name), 0:30], w1[r:r + 64, j, :],
                                          cmp_blocks[r:r + 64, j // 16, :, :, j % 16], start=(j == 0), stop=(j == 31))
                xpose.filled(mm, name)
            normed.wait(pe, "dk")
            for j in range(2):
                turn_pair(f"dk{j}", lambda a, t: rows[:, t, 3072 + (2 * j + a) * P:3072 + (2 * j + a + 1) * P])
            project("m_qg1", h_t)
            normed.wait(pe, "hid")
            xpose.claim(pe, "kvc")
            for c in range(2):
                for g in range(2):
                    at = (2 * c + g) * 64
                    mm = nc.tensor.matmul(psum[0:N_CMP, XPOSE_BANK + xpose.slot("kvc"), at:at + 64],
                                          hid[:, c, g * N_CMP:(g + 1) * N_CMP], E("cmp_w2")[:, c * 64:(c + 1) * 64],
                                          start=True, stop=True)
            xpose.filled(mm, "kvc")
            normed.wait(pe, "kc")
            xpose.claim(pe, "kc")
            for g in range(2):
                mm = nc.tensor.transpose(psum[:, XPOSE_BANK + xpose.slot("kc"), g * 16:(g + 1) * 16],
                                         kc_rows[0:16, g].rearrange("p a d -> p (a d)"), ident[0:16, 0:16])
            xpose.filled(mm, "kc")
            normed.wait(pe, "mq1")
            turn_pair("mq1", lambda a, t: rows[:, t, 1536 + a * P:1536 + (a + 1) * P])
            turned(pe, "dq0", "dq1", "dk0", "dk1", "kc", "mq1")
            chunk_read(pe, "dkv2")

            def operands1(u):
                r, g = 64 * (u.head % 2), u.head // 4
                if u.kind == "mem":
                    return (mq_t[r:r + 64, u.head // 2, :], mk_t[r:r + 64, 1, u.head // 2, :],
                            lambda kb: mkv[:, 1, kb, 256 + 64 * u.head:320 + 64 * u.head], 64 * u.head, True, True)
                if u.kind == "cmp":
                    k, v = kc_t[r:r + 64, g, :], lambda kb: kvc[0:16, 1, g, :]
                else:
                    j = 2 * (u.kind == "win") + g
                    k, v = k_t[r:r + 64, j, :], lambda kb: rows[:, kb, 1024 + 64 * j:1024 + 64 * (j + 1)]
                return q_t[r:r + 64, u.head // 2, :], k, v, 64 * u.head, u.kind == "cmp", u.kind == "win"

            layer_units(UNITS1, len(UNITS0), operands1, L1_FILL, {0: "diff", 4: "mem1"})
            normed.wait(pe, "conv")
            for t in range(T):
                xpose.claim(pe, f"yc{t}")
                for f in range(4):
                    mm = nc.tensor.transpose(psum[:, XPOSE_BANK + xpose.slot(f"yc{t}"), f * P:(f + 1) * P],
                                             conv_out[:, f, t * P:(t + 1) * P], ident)
                xpose.filled(mm, f"yc{t}")
            normed.wait(pe, "y_m1")
            turn_pair("ym1", lambda a, t: rows[:, t, 1792 + a * P:1792 + (a + 1) * P])
            normed.wait(pe, "y_d")
            for j in range(2):
                turn_pair(f"yb1_{j}", lambda a, t: rows[:, t, 2560 + (2 * j + a) * P:2560 + (2 * j + a + 1) * P])
            normed.wait(pe, "y_c")
            for j in range(2):
                turn_pair(f"ya1_{j}", lambda a, t: rows[:, t, 3072 + (2 * j + a) * P:3072 + (2 * j + a + 1) * P])
            out_project(1)

            normed.wait(pe, "x2")
            for j in range(4):
                turn_pair(f"x2_{j}", lambda a, t: h_rows[:, t, (2 * j + a) * P:(2 * j + a + 1) * P])
            turned(pe, "x2_2", "x2_3")

            def project_features(name, src):
                for half in range(2):
                    for _ in features_piece(name, half, src):
                        pass

            project_features("x_lru0", h_t)
            project_features("x_lru1", h_t)
            project("r_q", h_t)
            project("r_k", h_t)
            project_features("y_lru0", h_t)
            project_features("y_lru1", h_t)
            for c, name in enumerate(("rq", "rk")):
                normed.wait(pe, name)
                for j in range(2):
                    turn_pair(f"{name}{j}", lambda a, t: rows[:, t, c * 512 + (2 * j + a) * P:c * 512 + (2 * j + a + 1) * P])
            normed.wait(pe, "xc")
            wait_block(pe, "lru_w")
            lru_w = weights[:, block_index["lru_w"] % SLOTS, :].rearrange("p (c b k j) -> p c b k j", c=2, b=4, k=2)
            for b in range(4):
                for c, name in enumerate("ri"):
                    proj.claim(pe, (f"lru_{name}", b))
                    bank = psum[:, PROJ_BANK + proj.slot((f"lru_{name}", b)), :]
                    for j in range(2):
                        for k in range(2):
                            mm = nc.tensor.matmul(bank[:, j * S:(j + 1) * S], lru_w[:, c, b, k, j * P:(j + 1) * P],
                                                  y_t[:, 2 * b + k, :], start=(k == 0), stop=(k == 1))
                    proj.filled(mm, (f"lru_{name}", b))
            project("r_v0", h_t)
            project("r_v1", h_t)
            turned(pe, "rq0", "rq1", "rk0", "rk1")
            chunk_read(pe, "r_v0")
            chunk_read(pe, "r_v1")

            def retention_scores(h):
                i = n_units + h
                score.claim(pe, i)
                bank = psum[:, SCORE_BANK + score.slot(i), :]
                nc.tensor.matmul(bank[:, 0:S], k_t[:, h, 0:P], q_t[:, h, :], start=True, stop=True)
                score.filled(nc.tensor.matmul(bank[:, S:S + P], k_t[:, h, P:S], q_t[:, h, P:S], start=True, stop=True), i)

            def retention_values(h):
                pe.wait_ge(ret_decayed, h + 1)
                xpose.claim(pe, ("ret", h))
                bank = psum[:, XPOSE_BANK + xpose.slot(("ret", h)), :]
                v = [rows[:, t, 1024 + S * h:1024 + S * (h + 1)] for t in range(T)]
                s_t = probs_t[:, h % 2, :]
                nc.tensor.matmul(bank[:, 0:S], s_t[:, 0:P], v[0], start=True, stop=True)
                nc.tensor.matmul(bank[:, S:2 * S], s_t[:, P:2 * P], v[0], start=True, stop=False)
                xpose.filled(nc.tensor.matmul(bank[:, S:2 * S], s_t[:, 2 * P:3 * P], v[1], start=False, stop=True),
                             ("ret", h))

            retention_scores(0)
            for h in range(RET_HEADS):
                if h + 1 < RET_HEADS:
                    retention_scores(h + 1)
                retention_values(h)
            project("g_ret0", h_t)
            project("g_ret1", h_t)
            project_features("gate_r0", h_t)
            project_features("gate_l0", h_t)
            normed.wait(pe, "g_ret")
            for j in range(4):
                turn_pair(f"ret_y{j}", lambda a, t: h_rows[:, t, (2 * j + a) * P:(2 * j + a + 1) * P])

            class Tiles:
                def __getitem__(self, at):
                    return tile_of(0, at[1])

            for b in range(2):
                if b == 1:
                    project_features("gate_r1", h_t)
                    project_features("gate_l1", h_t)
                turned(pe, "ret_y2", "ret_y3")
                project_features(f"ret_o{b}", Tiles())
                normed.wait(pe, "lru_y")
                project_features(f"lru_o{b}", y_t)
            normed.wait(pe, "mix")
            for b in range(2):
                wait_block(pe, f"mix_out{b}")
                w = block_view(f"mix_out{b}")
                for t in range(T):
                    proj.claim(pe, (f"mix_out{b}", t))
                    for k in range(KT):
                        mm = nc.tensor.matmul(psum[:, PROJ_BANK + proj.slot((f"mix_out{b}", t)), :],
                                              tile_of(1024, k)[:, t * P:(t + 1) * P], w[:, k, :],
                                              start=(k == 0), stop=(k == KT - 1))
                    proj.filled(mm, (f"mix_out{b}", t))

            normed.wait(pe, "x3")
            for j in range(4):
                turn_pair(f"x3_{j}", lambda a, t: h_rows[:, t, (2 * j + a) * P:(2 * j + a + 1) * P])
            turned(pe, "x3_2", "x3_3")

            def ffn_down(i):
                pe.wait_ge(ffn_ready, 2 * (i + 1))
                wait_block(pe, f"down{i}")
                w = block_view(f"down{i}", D)
                hidden = rows[:, i % 2, 1024:2048].rearrange("p (k s) -> p k s", s=S)
                for k in range(4):
                    for t in range(T):
                        for half in range(2):
                            mm = nc.tensor.matmul(psum[:, 4 + 2 * t + half, :], hidden[:, k, t * P:(t + 1) * P],
                                                  w[:, k, half * CH:(half + 1) * CH],
                                                  start=(i == 0 and k == 0), stop=(i == FFN_STEPS - 1 and k == 3))
                mm.then_inc(down_done, 1)

            for i in range(FFN_STEPS):
                project_features(f"up_g{i}", h_t)
                project_features(f"up_v{i}", h_t)
                if i >= 1:
                    ffn_down(i - 1)
            ffn_down(FFN_STEPS - 1)

        @block_.scalar
        def _(act):
            link = Chain(act, act_chain)

            def square_sums(name, src):
                for t in range(T):
                    ins = nc.scalar.activation(act_tmp[:, :, :].rearrange("p a n -> p (a n)"), src[:, t, 0:D], ACT.Square,
                                               accum_out=x_sums[:, squares.done, t:t + 1])
                    if t == 0:
                        link(ins)
                squares.mark(ins, name, act)

            def copy_chunk(name, dst, cols=CH):
                for t in range(T):
                    proj.arrived(act, (name, t))
                    proj.freed(nc.scalar.activation(dst(t), psum[:, PROJ_BANK + proj.slot((name, t)), 0:cols], ACT.Copy),
                               (name, t), act)

            def unit_exp(i, u):
                act.wait_ge(logits_ready, i + 1)
                for t in range(T):
                    ins = nc.scalar.activation(logits[:, i % 3, u.seg(t)], logits[:, i % 3, u.seg(t)], ACT.Exp,
                                               bias=neg_max[:, i % 2, t:t + 1], scale=-1.0,
                                               accum_out=row_sum[:, i % 2, t:t + 1])
                ins.then_inc(exp_done, 1)
                act.wait_ge(exp_done, i + 1)

            def unit_evac(i, u):
                xpose.arrived(act, ("unit", i))
                if i >= 2:
                    act.wait_ge(pv_done, i - 1)
                n = len(u.blocks) * P
                keys = min(P, u.keys[0])
                xpose.freed(nc.scalar.activation(probs_t[0:keys, i % 2, 0:n],
                                                 psum[0:keys, XPOSE_BANK + xpose.slot(("unit", i)), 0:n], ACT.Copy),
                            ("unit", i), act)

            act.wait_ge(loaded["mem"], 16)
            square_sums("mem", rows)
            act.wait_ge(sin_args, 1)
            link(nc.scalar.activation(cos2[:, :], cos2[:, :], ACT.Sin))
            nc.scalar.activation(sin2[:, :], sin2[:, :], ACT.Sin).then_inc(sin_ready, 1)
            act.wait_ge(sin_ready, 1)
            act.wait_ge(loaded["x"], 16)
            square_sums("x0", x)
            copy_chunk("kv0", lambda t: mkv[:, 0, t, :])
            copy_chunk("kv1", lambda t: mkv[:, 1, t, :])
            act.wait_ge(lam_dots, 1)
            nc.scalar.activation(lam_tmp[:, 2:4], lam_tmp[:, 0:2], ACT.Exp).then_inc(lam_exp, 1)
            act.wait_ge(lam_exp, 1)
            copy_chunk("b_q", lambda t: rows[:, t, 1536:2048])
            copy_chunk("b_k", lambda t: rows[:, t, 2048:2560])
            copy_chunk("m_qg0", lambda t: rows[:, t, 3584:4096])

            chunk_read(act, "m_qg0")
            gate_m.mark(nc.scalar.activation(gate_tmp[:, :, :], rows[:, :, 3840:4096], ACT.Tanh, scale=0.5), 0, act)
            copy_chunk("b_v", lambda t: rows[:, t, 2560:3072])

            def fill_half(layer, p, name, gelu):
                proj.arrived(act, name)
                if layer == 1 and p < 2:
                    proj.freed(nc.scalar.activation(rows[:, p, 3584:4096], psum[:, PROJ_BANK + proj.slot(name), :],
                                                    ACT.Tanh, scale=0.5), name, act)
                    return
                if layer == 1 and p < 4:
                    return
                if p >= 2:
                    proj.read(act, (([L0_FILL, L1_FILL][layer])[(p - 2) // 2], p % 2))
                src = psum[:, PROJ_BANK + proj.slot(name), :]
                if gelu:
                    fill_act.mark(nc.scalar.activation(act_tmp[:, p % 2, :], src, ACT.Square), (layer, "square", p), act)
                else:
                    fill_act.mark(nc.scalar.activation(act_tmp[:, p % 2, :], src, ACT.Tanh, scale=0.5),
                                  (layer, "tanh", p), act)

            def fill_tanh(layer, p):
                fill_poly.wait(act, (layer, p))
                fill_act.mark(nc.scalar.activation(act_tmp[:, p % 2, :], act_tmp[:, p % 2, :], ACT.Tanh, scale=GELU_C),
                              (layer, "tanh", p), act)

            def layer_units(layer, units, base, fill, groups):
                n = len(units)
                for i in range(n + 2):
                    if i < n:
                        unit_exp(base + i, units[i])
                        for p in pieces_at(i, n):
                            gelu = layer == 0 and p < 4
                            fill_half(layer, p, (fill[p // 2], p % 2), gelu)
                            if gelu:
                                fill_tanh(layer, p)
                    if 1 <= i <= n:
                        unit_evac(base + i - 1, units[i - 1])
                    for last, name, dst, width in groups:
                        if i == last + 2:
                            act.wait_ge(pv_done, base + last + 1)
                            for t in range(T):
                                ins = nc.scalar.activation(dst(t), psum[:, OUT_BANK + t, 0:width], ACT.Copy)
                            heads_out.mark(ins, name, act)

            layer_units(0, UNITS0, 0, L0_FILL,
                        [(3, "mem0", lambda t: rows[:, t, 3584:3840], 256),
                         (19, "diff", lambda t: rows[:, t, 1536:2048], 512)])

            def turn_y(name, tile0, scale):
                xpose.arrived(act, name)
                xpose.freed(nc.scalar.activation(y_t[:, tile0:tile0 + 2, :],
                                                 psum[:, XPOSE_BANK + xpose.slot(name), :], ACT.Copy, scale=scale), name, act)

            turn_y("ym0", 8, 0.5)
            turn_y("ya0_0", 0, 0.25)
            turn_y("ya0_1", 2, 0.25)
            turn_y("yb0_0", 4, 0.5 * (1.0 - LAM_INIT))
            turn_y("yb0_1", 6, 0.5 * (1.0 - LAM_INIT))

            x_ready.wait(act, "x1")
            square_sums("x1", x)
            copy_chunk("d_q", lambda t: rows[:, t, 0:512])
            copy_chunk("dkv1", lambda t: rows[:, t, 512:1024])
            copy_chunk("dkv2", lambda t: rows[:, t, 1024:1304], 280)
            nc.scalar.activation(gates[:, :, :], rows[:, :, 1280:1304], ACT.Tanh, scale=0.5).then_inc(gates_tanh, 1)
            act.wait_ge(gates_tanh, 1)
            for j, name in enumerate("kv"):
                xpose.arrived(act, f"hid_{name}")
                hid_tanh.mark(nc.scalar.activation(hid_tmp[:, j, :],
                                                   psum[:, XPOSE_BANK + xpose.slot(f"hid_{name}"), 0:30],
                                                   ACT.Tanh, scale=0.5), name, act)
            copy_chunk("m_qg1", lambda t: rows[:, t, 1536:2048])
            gate_m.mark(nc.scalar.activation(gate_tmp[:, :, :], rows[:, :, 1792:2048], ACT.Tanh, scale=0.5), 1, act)
            layer_units(1, UNITS1, len(UNITS0), L1_FILL,
                        [(3, "mem1", lambda t: rows[:, t, 1536:1792], 256),
                         (27, "nsa", lambda t: rows[:, t, 0:512], 512)])
            turn_y("ym1", 8, 0.5)
            turn_y("yb1_0", 4, 0.5)
            turn_y("yb1_1", 6, 0.5)
            act.wait_ge(yc_normed, 1)
            nc.scalar.activation(act_tmp[:, :, :], rows[:, :, 3072:3584], ACT.Tanh, scale=0.5).then_inc(yc_tanh, 1)
            act.wait_ge(yc_tanh, 1)
            act.dma_start(late, late_d).then_inc(loaded["late"], 16)
            turn_y("ya1_0", 0, 0.25)
            turn_y("ya1_1", 2, 0.25)

            x_ready.wait(act, "x2")
            square_sums("x2", x)

            def copy_features(name, c0, i0, func=ACT.Copy):
                for half in range(2):
                    proj.arrived(act, (name, half))
                    proj.freed(nc.scalar.activation(pair_of(c0, i0 + half),
                                                    psum[:, PROJ_BANK + proj.slot((name, half)), :], func),
                               (name, half), act)

            act.wait_ge(lam_neg, 1)
            nc.scalar.activation(lam_exp_in[:, :], lam_exp_in[:, :], ACT.Exp).then_inc(lam_neg_exp, 1)
            act.wait_ge(lam_neg_exp, 1)
            copy_features("x_lru0", 3072, 0)
            copy_features("x_lru1", 3072, 2)
            copy_chunk("r_q", lambda t: rows[:, t, 0:512])
            copy_chunk("r_k", lambda t: rows[:, t, 512:1024])
            copy_features("y_lru0", 2048, 0, ACT.Gelu_apprx_tanh)
            copy_features("y_lru1", 2048, 2, ACT.Gelu_apprx_tanh)
            act.wait_ge(lru_coef, 1)
            for b in range(4):
                for c, name in enumerate("ri"):
                    use = (f"lru_{name}", b)
                    proj.arrived(act, use)
                    if name == "i" and b >= 2:
                        act.wait_ge(lru_in, b - 1)
                    for j in range(2):
                        f = 2 * b + j
                        dst = tile_of(3072, f) if name == "r" else act_tmp[:, b % 2, j * S:(j + 1) * S]
                        ins = nc.scalar.activation(dst, psum[:, PROJ_BANK + proj.slot(use), j * S:(j + 1) * S],
                                                   ACT.Tanh, scale=0.5, bias=half_bias[:, c * KT + f:c * KT + f + 1])
                    proj.freed(ins, use, act)
                for j in range(2):
                    f = 2 * b + j
                    link(nc.scalar.activation(h_rows[:, f // 4, S * (f % 4):S * (f % 4 + 1)], tile_of(3072, f), ACT.Exp,
                                              scale=decay_coef[:, 1, f:f + 1], bias=decay_coef[:, 1, f:f + 1]))
                    ins = nc.scalar.activation(tile_of(3072, f), tile_of(3072, f), ACT.Tanh,
                                               scale=decay_coef[:, 0, f:f + 1], bias=decay_coef[:, 0, f:f + 1])
                ins.then_inc(lru_exp, 1)
                act.wait_ge(lru_exp, b + 1)
            act.wait_ge(lru_ratio, 1)
            nc.scalar.activation(rows[:, :, 3072:4096], rows[:, :, 3072:4096], ACT.Sqrt, scale=0.5).then_inc(lru_root, 1)
            act.wait_ge(lru_root, 1)
            copy_chunk("r_v0", lambda t: rows[:, t, 1024:1536])
            copy_chunk("r_v1", lambda t: rows[:, t, 1536:2048])
            normed.wait(act, "lru_y")
            for h in range(RET_HEADS):
                xpose.arrived(act, ("ret", h))
                for t in range(T):
                    ins = nc.scalar.activation(h_rows[:, t, S * h:S * (h + 1)],
                                               psum[:, XPOSE_BANK + xpose.slot(("ret", h)), t * S:(t + 1) * S],
                                               ACT.Identity, accum_out=head_sums[:, t, h:h + 1])
                xpose.freed(ins, ("ret", h), act)
            for b in range(2):
                for t in range(T):
                    n = 2 * b + t
                    proj.arrived(act, (f"g_ret{b}", t))
                    if n >= 2:
                        proj.read(act, (f"g_ret{b - 1}", t))
                    nc.scalar.activation(act_tmp[:, n % 2, :], psum[:, PROJ_BANK + proj.slot((f"g_ret{b}", t)), :],
                                         ACT.Tanh, scale=0.5).then_inc(g_tanh, 1)
                    act.wait_ge(g_tanh, n + 1)
            n = 0
            for b in range(2):
                for c, (name, c0) in enumerate((("gate_r", 1024), ("gate_l", 2048))):
                    if (b, c) == (0, 1):
                        normed.wait(act, "g_ret")
                    for half in range(2):
                        use = (f"{name}{b}", half)
                        proj.arrived(act, use)
                        for a in range(2):
                            f = 4 * b + 2 * half + a
                            ins = nc.scalar.activation(
                                tile_of(c0, f), psum[:, PROJ_BANK + proj.slot(use), a * S:(a + 1) * S], ACT.Tanh,
                                scale=0.5, bias=half_bias[:, (2 + c) * KT + f:(2 + c) * KT + f + 1])
                        proj.freed(ins, use, act)

            x_ready.wait(act, "x3")
            square_sums("x3", x)
            for i in range(FFN_STEPS):
                for half in range(2):
                    act.wait_ge(conv_gate, 2 * i + half + 1)
                    part = rows[:, i % 2, 512 * half:512 * (half + 1)]
                    nc.scalar.activation(part, part, ACT.Gelu_apprx_tanh).then_inc(conv_gelu, 1)
                    act.wait_ge(conv_gelu, 2 * i + half + 1)
            x_ready.wait(act, "final")
            square_sums("final", x)

        @block_.vector
        def _(vec):
            link = Chain(vec, vec_chain)
            V = nc.vector

            def spread(ap, shape, axis):
                return ap.unsqueeze(axis).broadcast_to(shape)

            def scale_from(name, sums, count, factor=1.0):
                n = mean_ready.names.index(name)
                width = NORMS[n][1]
                p = sums.shape[0]
                mean_ready.mark(V.tensor_scalar(mean_sq[0:p, n % 2, 0:width], sums, factor * factor / count, EPS,
                                                ALU.mult, ALU.add), name, vec)
                rstd_ready.wait(vec, name)
                return rstd[0:p, n % 2, 0:width]

            def grouped_norm(name, src, gain, factor=1.0):
                p, a, g, d = src.shape
                sq = scratch[0:p, 0:a * g * d].rearrange("p (a g d) -> p a g d", a=a, g=g)
                link(V.tensor_tensor(sq, src, src, ALU.mult))
                link(V.tensor_reduce(sumsq[0:p, 0:a * g], scratch[0:p, 0:a * g * d].rearrange("p (a d) -> p a d", d=d),
                                     AX_X, ALU.add))
                r = scale_from(name, sumsq[0:p, 0:a * g], d, factor)
                link(V.tensor_tensor(src, src, spread(r.rearrange("p (a g) -> p a g", a=a), [p, a, g, d], 3), ALU.mult))
                for t in range(a):
                    wide = gain if len(gain.shape) == 3 else spread(gain, [p, g, d], 1)
                    ins = V.scalar_tensor_tensor(src[:, t], src[:, t], factor, wide, ALU.mult, ALU.mult)
                return ins

            def rope(src, cos, sin, half, tmp=None):
                p, a, g, d = src.shape
                shape = [p, a, g, half]
                tmp = rope_tmp if tmp is None else tmp
                tmp = [tmp[0:p, j, 0:a * g * half].rearrange("p (a g h) -> p a g h", a=a, g=g) for j in range(4)]
                c, s_ = (spread(v.rearrange("p (a h) -> p a h", a=a), shape, 2) for v in (cos, sin))
                x1, x2 = src[:, :, :, 0:half], src[:, :, :, half:2 * half]
                V.tensor_tensor(tmp[0], x1, c, ALU.mult)
                V.tensor_tensor(tmp[1], x2, s_, ALU.mult)
                V.tensor_tensor(tmp[2], x1, s_, ALU.mult)
                link(V.tensor_tensor(tmp[3], x2, c, ALU.mult))
                link(V.tensor_tensor(x1, tmp[0], tmp[1], ALU.subtract))
                return V.tensor_tensor(x2, tmp[2], tmp[3], ALU.add)

            def heads(base, c0, g, d):
                return base[:, :, c0:c0 + g * d].rearrange("p t (g d) -> p t g d", d=d)

            def turn_in(name, dst, gain=None):
                xpose.arrived(vec, name)
                src = psum[:, XPOSE_BANK + xpose.slot(name), :].rearrange("p (a s) -> p a s", a=2)
                if gain is None:
                    ins = V.tensor_copy(dst, src)
                else:
                    ins = V.tensor_tensor(dst, src, spread(gain, [P, 2, S], 2), ALU.mult)
                xpose.freed(ins, name, vec)

            def norm_rows(name, src, dst):
                squares.wait(vec, name)
                r = scale_from(name, x_sums[:, squares.names.index(name), :], D)
                for t in range(T):
                    ins = V.tensor_scalar(dst[:, t, 0:D], src[:, t, 0:D], r[:, t:t + 1], None, ALU.mult)
                normed.mark(ins, name, vec)

            vec.wait_ge(loaded["early"], 16)
            vec.wait_ge(loaded["positions"], 16)
            pos_f, ang, turns = rope_tmp[:, 0, 0:T], rope_tmp[:, 1, :], rope_tmp[:, 2, :]
            link(V.tensor_copy(pos_f, positions[:, :]))
            for t in range(T):
                link(V.tensor_scalar(ang[:, t * 64:(t + 1) * 64], E("inv_freq"), pos_f[:, t:t + 1], None, ALU.mult))
            for shift, dst in ((0.25, cos2), (0.0, sin2)):
                link(V.tensor_scalar(turns, ang, float(1 / (2 * np.pi)), shift, ALU.mult, ALU.add))
                link(V.tensor_scalar(turns, turns, ROUND, ROUND, ALU.add, ALU.subtract))
                link(V.scalar_tensor_tensor(dst[:, :], turns, -TWO_PI_PARTS[0], ang, ALU.mult, ALU.add))
                for part in TWO_PI_PARTS[1:]:
                    link(V.scalar_tensor_tensor(dst[:, :], turns, -part, dst[:, :], ALU.mult, ALU.add))
                link(V.tensor_scalar(dst[:, :], dst[:, :], 2 * np.pi * shift, PI_BELOW, ALU.add, ALU.min))
                ins = V.tensor_scalar(dst[:, :], dst[:, :], -PI_BELOW, None, ALU.max)
                if shift:
                    link(ins)
            ins.then_inc(sin_args, 1)
            vec.wait_ge(sin_args, 1)
            link(V.memset(lam_tmp[:, :], 0.0))
            norm_rows("mem", rows, rows)
            for j in range(4):
                turn_in(f"mem{j}", y_t[:, 2 * j:2 * j + 2, :], E("mem_norm")[:, 2 * j:2 * j + 2])
            norm_rows("x0", x, h_rows)
            for j in range(4):
                turn_in(f"x0_{j}", h_t[:, 2 * j:2 * j + 2, :], E("l0_norm")[:, 2 * j:2 * j + 2])
            ws = [a.rearrange("p (g t) -> p g t", g=4) for a in (ws_masked[:, :], E("a_ws_t"))]
            V.tensor_tensor(ws[0], ws[1], spread(E("tril_t"), [P, 4, P], 1), ALU.mult).then_inc(ws_ready, 1)
            vec.wait_ge(ws_ready, 1)
            for j, (a, b) in enumerate((("b_lq1", "b_lk1"), ("b_lq2", "b_lk2"))):
                link(V.tensor_tensor(scratch[:, 0:32], E(a), E(b), ALU.mult))
                ins = V.tensor_reduce(lam_tmp[:, j:j + 1], scratch[:, 0:32], AX_X, ALU.add)
                if j == 0:
                    link(ins)
            ins.then_inc(lam_dots, 1)
            vec.wait_ge(lam_dots, 1)
            for l in range(2):
                chunk_read(vec, f"kv{l}")
                normed.mark(grouped_norm(f"mk{l}", heads(mkv[:, l], 0, 4, 64), E(f"m{l}_knorm")), f"mk{l}", vec)
            vec.wait_ge(lam_exp, 1)
            link(V.tensor_tensor(lam_tmp[:, 4:5], lam_tmp[:, 3:4], lam_tmp[:, 2:3], ALU.subtract))
            for t in range(T):
                link(V.tensor_scalar(coef[:, t:t + 1], lam_tmp[:, 4:5], LAM_INIT, None, ALU.subtract))
            for l in range(2):
                turn_in(f"mk{l}", mk_t[:, l])
            for j, (name, c0, gain, dst) in enumerate((("q", 1536, "b_qnorm", q_t), ("k", 2048, "b_knorm", k_t))):
                chunk_read(vec, "b_" + name)
                v = heads(rows, c0, 16, 32)
                link(grouped_norm(name, v, E(gain)))
                normed.mark(rope(v, E("cos0"), E("sin0"), 4), name, vec)
                for j in range(2):
                    turn_in(f"{name}{j}", dst[:, 2 * j:2 * j + 2, :])
            chunk_read(vec, "m_qg0")
            normed.mark(grouped_norm("mq0", heads(rows, 3584, 4, 64), E("m0_qnorm")), "mq0", vec)
            gate_m.wait(vec, 0)
            link(V.scalar_tensor_tensor(rows[:, :, 3840:4096], gate_tmp[:, :, :], 1.0, rows[:, :, 3840:4096],
                                        ALU.add, ALU.mult))
            turn_in("mq0", mq_t[:, :, :])

            def unit_logits(i, u):
                score.arrived(vec, i)
                if i >= 3:
                    xpose.arrived(vec, ("unit", i - 3))
                src = psum[:, SCORE_BANK + score.slot(i), 0:u.width]
                e = logits[:, i % 3, 0:u.width]
                if u.kind == "mem":
                    ins = V.tensor_scalar(e, src, -u.scale, None, ALU.mult)
                else:
                    mask = E("cmp_mask") if u.kind == "cmp" else E("causal")
                    ins = V.scalar_tensor_tensor(e, src, -u.scale, mask, ALU.mult, ALU.add)
                score.freed(ins, i, vec)
                score.read(vec, i)
                if u.keys[0] == u.keys[1]:
                    ins = V.tensor_reduce(neg_max[:, i % 2, :], e.rearrange("p (t k) -> p t k", t=T), AX_X, ALU.min)
                else:
                    for t in range(T):
                        ins = V.tensor_reduce(neg_max[:, i % 2, t:t + 1], logits[:, i % 3, u.seg(t)], AX_X, ALU.min)
                ins.then_inc(logits_ready, 1)
                vec.wait_ge(logits_ready, i + 1)

            def unit_probs(i, u, factor):
                vec.wait_ge(exp_done, i + 1)
                w = row_inv
                link(V.reciprocal(row_inv[:, :], row_sum[:, i % 2, :]))
                if factor is not None:
                    link(V.tensor_tensor(row_scale[:, :], row_inv[:, :], factor, ALU.mult))
                    w = row_scale
                for t in range(T):
                    e = logits[:, i % 3, u.seg(t)]
                    ins = V.tensor_scalar(e, e, w[:, t:t + 1], None, ALU.mult)
                ins.then_inc(probs_ready, 1)
                vec.wait_ge(probs_ready, i + 1)

            def fill_piece(layer, p, name, dst, gelu):
                src = psum[:, PROJ_BANK + proj.slot(name), :]
                tmp = act_tmp[:, p % 2, :]
                if gelu:
                    fill_act.wait(vec, (layer, "square", p))
                    link(V.tensor_scalar(tmp, tmp, GELU_A, 1.0, ALU.mult, ALU.add))
                    fill_poly.mark(V.tensor_tensor(tmp, tmp, src, ALU.mult), (layer, p), vec)
                fill_act.wait(vec, (layer, "tanh", p))
                proj.freed(V.scalar_tensor_tensor(dst, tmp, 1.0, src, ALU.add, ALU.mult), name, vec)

            def layer_units(layer, units, base, fill, factor, piece, extra):
                n = len(units)
                for i in range(n + 2):
                    if i < n:
                        unit_logits(base + i, units[i])
                    if 1 <= i <= n:
                        unit_probs(base + i - 1, units[i - 1], factor(units[i - 1]))
                    if i < n:
                        for p in pieces_at(i, n):
                            piece(p)
                    extra(i)

            FILL0_COL = {"a_v": 512, "a_u": 0, "a_g": 1024, "b_g": 3072}

            def piece0(p):
                name, t = L0_FILL[p // 2], p % 2
                fill_piece(0, p, (name, t), rows[:, t, FILL0_COL[name]:FILL0_COL[name] + 512], p < 4)
                if p == 1:
                    chunk_read(vec, "a_v")
                    normed.mark(grouped_norm("a_v", heads(rows, 512, 4, P),
                                             E("a_vnorm").rearrange("p (g d) -> p g d", d=P), 0.5), "a_v", vec)
                if p == 5:
                    chunk_read(vec, "a_g")
                    link(V.tensor_tensor(rows[:, :, 0:512], rows[:, :, 0:512], rows[:, :, 1024:1536], ALU.mult))

            layer_units(0, UNITS0, 0, L0_FILL, lambda u: coef[:, :] if (u.kind, u.sub) == ("diff", 1) else None,
                        piece0, lambda i: None)
            heads_out.wait(vec, "mem0")
            normed_ym = V.tensor_tensor(rows[:, :, 3840:4096], rows[:, :, 3584:3840], rows[:, :, 3840:4096], ALU.mult)
            normed.mark(normed_ym, "y_m0", vec)
            for t in range(T):
                xpose.arrived(vec, f"z{t}")
                for g in range(4):
                    c = slice(g * P, (g + 1) * P)
                    ins = V.scalar_tensor_tensor(rows[:, t, c], psum[:, XPOSE_BANK + xpose.slot(f"z{t}"), c],
                                                 E("a_bs")[:, g:g + 1], rows[:, t, c], ALU.add, ALU.mult)
                xpose.freed(ins, f"z{t}", vec)
            for t in range(T):
                xpose.read(vec, f"z{t}")
            normed.mark(V.memset(lam_tmp[:, 7:8], 0.0), "y_a0", vec)
            heads_out.wait(vec, "diff")
            o = heads(rows, 1536, 8, 64)
            link(grouped_norm("y_b", o, E("b_subln")))
            normed.mark(V.tensor_tensor(rows[:, :, 3072:3584], rows[:, :, 3072:3584], rows[:, :, 1536:2048], ALU.mult),
                        "y_b", vec)

            def residual(layer):
                for half, name in enumerate((f"out{layer}_a", f"out{layer}_b")):
                    for t in range(T):
                        proj.arrived(vec, (name, t))
                        part = x[:, t, half * CH:(half + 1) * CH]
                        proj.freed(V.tensor_tensor(part, psum[:, PROJ_BANK + proj.slot((name, t)), :], part, ALU.add),
                                   (name, t), vec)

            residual(0)
            chunk_read(vec, "out0_b")
            x_ready.mark(V.memset(lam_tmp[:, 7:8], 0.0), "x1", vec)

            link(V.memset(kvc[:, :, :, :], 0.0))
            link(V.memset(kc_rows[:, :, :, :], 0.0))
            link(V.memset(conv_in[:, :, :], 0.0))
            norm_rows("x1", x, h_rows)
            for j in range(4):
                turn_in(f"x1_{j}", h_t[:, 2 * j:2 * j + 2, :], E("l1_norm")[:, 2 * j:2 * j + 2])
            chunk_read(vec, "d_q")
            dq = heads(rows, 0, 8, 64)
            link(grouped_norm("dq", dq, E("d_qnorm")))
            normed.mark(rope(dq, E("cos1"), E("sin1"), 8), "dq", vec)
            chunk_read(vec, "dkv1")
            dk = heads(rows, 768, 4, 64)
            link(grouped_norm("dk", dk, E("d_knorm")))
            link(rope(dk, E("cos1"), E("sin1"), 8))
            for t in range(T):
                pair = rows[:, t, 3072:3584].rearrange("p (g c d) -> p g c d", c=2, d=64)
                for c in range(2):
                    ins = V.tensor_copy(pair[:, :, c, :], dk[:, t])
                    if (t, c) != (1, 1):
                        link(ins)
            normed.mark(ins, "dk", vec)
            xpose.arrived(vec, "cmp")
            bank = psum[:, XPOSE_BANK + xpose.slot("cmp"), :]
            for g in range(2):
                for jh in range(2):
                    at = g * S + 16 * jh
                    ins = V.tensor_tensor(cmp_blocks[:, jh, g], bank[:, at:at + 240].rearrange("p (n j) -> p n j", j=16),
                                          spread(E("cmp_pos")[:, 16 * jh:16 * jh + 16], [P, N_CMP, 16], 1), ALU.add)
            xpose.freed(ins, "cmp", vec)
            normed.mark(V.memset(lam_tmp[:, 7:8], 0.0), "cmp_blocks", vec)
            for j in range(2):
                turn_in(f"dq{j}", q_t[:, 2 * j:2 * j + 2, :])
            vec.wait_ge(gates_tanh, 1)
            link(V.tensor_scalar(gates[:, :, :], gates[:, :, :], 0.5, 0.5, ALU.mult, ALU.add))
            first = gates[:, :, 0:24:3]
            link(V.tensor_tensor(first, first, spread(E("cmp_valid"), [P, T, 8], 2), ALU.mult))
            for j, name in enumerate("kv"):
                hid_tanh.wait(vec, name)
                xpose.freed(V.scalar_tensor_tensor(hid[:, j, :], hid_tmp[:, j, :], 1.0,
                                                   psum[:, XPOSE_BANK + xpose.slot(f"hid_{name}"), 0:30],
                                                   ALU.add, ALU.mult), f"hid_{name}", vec)
            normed.mark(V.memset(lam_tmp[:, 7:8], 0.0), "hid", vec)
            for j in range(2):
                turn_in(f"dk{j}", k_t[:, 2 * j:2 * j + 2, :])
            xpose.arrived(vec, "kvc")
            xpose.freed(V.tensor_scalar(kvc[0:N_CMP].rearrange("p a b c -> p (a b c)"),
                                        psum[0:N_CMP, XPOSE_BANK + xpose.slot("kvc"), 0:256], 0.5, None, ALU.mult),
                        "kvc", vec)
            kc = kvc[0:N_CMP, 0:1]
            link(grouped_norm("kc", kc, E("d_knorm", N_CMP)))
            link(rope(kc, E("cos_cmp", N_CMP), E("sin_cmp", N_CMP), 8))
            link(V.tensor_copy(kc_rows[0:N_CMP, :, 0, :], kc[:, 0]))
            normed.mark(V.tensor_copy(kc_rows[0:N_CMP, :, 1, :], kc[:, 0]), "kc", vec)
            chunk_read(vec, "m_qg1")
            normed.mark(grouped_norm("mq1", heads(rows, 1536, 4, 64), E("m1_qnorm")), "mq1", vec)
            xpose.arrived(vec, "kc")
            xpose.freed(V.tensor_copy(kc_t[:, :, :].rearrange("p g n -> p (g n)"),
                                      psum[:, XPOSE_BANK + xpose.slot("kc"), 0:32]), "kc", vec)
            gate_m.wait(vec, 1)
            link(V.scalar_tensor_tensor(rows[:, :, 1792:2048], gate_tmp[:, :, :], 1.0, rows[:, :, 1792:2048],
                                        ALU.add, ALU.mult))
            turn_in("mq1", mq_t[:, :, :])

            def piece1(p):
                name, t = L1_FILL[p // 2], p % 2
                if name == "c_b":
                    return
                if name == "c_a":
                    proj.read(vec, ("c_b", t))
                    proj.arrived(vec, (name, t))
                    proj.freed(V.scalar_tensor_tensor(
                        conv_in[:, 2 * t:2 * t + 2, 30:30 + S], rows[:, t, 3584:4096].rearrange("p (a s) -> p a s", a=2),
                        1.0, psum[:, PROJ_BANK + proj.slot((name, t)), :].rearrange("p (a s) -> p a s", a=2),
                        ALU.add, ALU.mult), (name, t), vec)
                else:
                    at = 2048 if name == "c_g" else 2560
                    fill_piece(1, p, (name, t), rows[:, t, at:at + 512], False)

            def conv_steps():
                for tap in range(31):
                    for f in range(4):
                        w = E("conv_w")[:, 31 * f + tap:31 * f + tap + 1]
                        src, dst = conv_in[:, f, tap:tap + S], conv_out[:, f, :]
                        if tap == 0:
                            ins = V.tensor_scalar(dst, src, w, None, ALU.mult)
                        else:
                            ins = V.scalar_tensor_tensor(dst, src, w, dst, ALU.mult, ALU.add)
                        if f == 3:
                            link(ins)
                        yield
                for f in range(4):
                    ins = V.tensor_scalar(conv_out[:, f, :], conv_out[:, f, :], 0.5, E("conv_b")[:, f:f + 1],
                                          ALU.mult, ALU.add)
                normed.mark(ins, "conv", vec)

            conv = conv_steps()
            conv_from = 1 + max(i for i in range(len(UNITS1)) if 3 in pieces_at(i, len(UNITS1)))

            def extra1(i):
                if i >= conv_from:
                    for _ in range(8):
                        next(conv, None)

            layer_units(1, UNITS1, len(UNITS0), L1_FILL,
                        lambda u: None if u.kind == "mem" else
                        gates[:, :, 3 * u.head + ("cmp", "slc", "win").index(u.kind)], piece1, extra1)
            for _ in conv:
                pass
            normed.mark(V.tensor_tensor(rows[:, :, 1792:2048], rows[:, :, 1536:1792], rows[:, :, 1792:2048], ALU.mult),
                        "y_m1", vec)
            heads_out.wait(vec, "nsa")
            normed.mark(V.tensor_tensor(rows[:, :, 2560:3072], rows[:, :, 2560:3072], rows[:, :, 0:512], ALU.mult),
                        "y_d", vec)
            for t in range(T):
                xpose.arrived(vec, f"yc{t}")
                xpose.freed(V.tensor_copy(rows[:, t, 3072:3584], psum[:, XPOSE_BANK + xpose.slot(f"yc{t}"), :]),
                            f"yc{t}", vec)
            yc = heads(rows, 3072, 1, 512)
            grouped_norm("y_c", yc, E("c_norm")).then_inc(yc_normed, 1)
            vec.wait_ge(yc_normed, 1)
            vec.wait_ge(yc_tanh, 1)
            link(V.scalar_tensor_tensor(rows[:, :, 3072:3584], act_tmp[:, :, :], 1.0, rows[:, :, 3072:3584],
                                        ALU.add, ALU.mult))
            normed.mark(V.tensor_tensor(rows[:, :, 3072:3584], rows[:, :, 3072:3584], rows[:, :, 2048:2560], ALU.mult),
                        "y_c", vec)
            residual(1)
            chunk_read(vec, "out1_b")
            x_ready.mark(V.memset(lam_tmp[:, 7:8], 0.0), "x2", vec)

            vec.wait_ge(loaded["late"], 16)
            norm_rows("x2", x, h_rows)
            for j in range(4):
                turn_in(f"x2_{j}", h_t[:, 2 * j:2 * j + 2, :], L("norm1")[:, 2 * j:2 * j + 2])
            for n, name in enumerate(("lru_b_r", "lru_b_i")):
                link(V.tensor_scalar(half_bias[:, n * KT:(n + 1) * KT], L(name), 0.5, None, ALU.mult))
            link(V.tensor_scalar(half_bias[:, 2 * KT:], L("merge_b"), 0.5, None, ALU.mult))
            link(V.tensor_scalar(L("ret_gn"), L("ret_gn"), 0.5, None, ALU.mult))
            y, z, z2, acc = (scratch[:, n * KT:(n + 1) * KT] for n in range(4))
            link(V.tensor_scalar(y, L("lru_lambda"), -1.0, None, ALU.mult))
            link(V.tensor_tensor(scratch[:, 4 * KT:5 * KT], y, L("lru_lambda"), ALU.min))
            link(V.tensor_scalar(scratch[:, 5 * KT:6 * KT], y, 0.0, None, ALU.max))
            V.tensor_copy(lam_exp_in[:, :], scratch[:, 4 * KT:5 * KT]).then_inc(lam_neg, 1)
            vec.wait_ge(lam_neg, 1)
            vec.wait_ge(lam_neg_exp, 1)
            y = lam_exp_in[:, :]
            link(V.tensor_scalar(z, y, 2.0, None, ALU.add))
            link(V.reciprocal(z, z))
            link(V.tensor_tensor(z, z, y, ALU.mult))
            link(V.tensor_tensor(z2, z, z, ALU.mult))
            link(V.memset(acc, 1.0 / 17))
            for odd in range(15, 0, -2):
                link(V.tensor_tensor(acc, acc, z2, ALU.mult))
                link(V.tensor_scalar(acc, acc, 1.0 / odd, None, ALU.add))
            link(V.tensor_tensor(acc, acc, z, ALU.mult))
            link(V.scalar_tensor_tensor(acc, acc, 2.0, scratch[:, 5 * KT:6 * KT], ALU.mult, ALU.add))
            link(V.tensor_scalar(decay_coef[:, 0, :], acc, 4.0, None, ALU.mult))
            V.tensor_scalar(decay_coef[:, 1, :], acc, -4.0, None, ALU.mult).then_inc(lru_coef, 1)
            vec.wait_ge(lru_coef, 1)
            for b in range(2):
                chunk_read(vec, f"x_lru{b}")
                for lag in range(4):
                    for f in range(4 * b, 4 * b + 4):
                        w = L("lru_conv_w")[:, 4 * f + 3 - lag:4 * f + 4 - lag]
                        if lag == 0:
                            ins = V.tensor_scalar(y_t[:, f, :], tile_of(3072, f), w, L("lru_conv_b")[:, f:f + 1],
                                                  ALU.mult, ALU.add)
                        else:
                            ins = V.scalar_tensor_tensor(y_t[:, f, lag:], tile_of(3072, f)[:, 0:S - lag], w,
                                                         y_t[:, f, lag:], ALU.mult, ALU.add)
                    if (b, lag) != (1, 3):
                        link(ins)
            normed.mark(ins, "xc", vec)
            vec.wait_ge(sin_ready, 1)
            wide = h_rows[:, :, :].rearrange("p t (a n) -> p (t a) n", a=2)
            for c, name in enumerate(("rq", "rk")):
                chunk_read(vec, "r_" + name[1])
                normed.mark(rope(heads(rows, c * 512, 4, P), cos2[:, :], sin2[:, :], 64, wide), name, vec)
            for c, (name, dst) in enumerate((("rq", q_t), ("rk", k_t))):
                for j in range(2):
                    turn_in(f"{name}{j}", dst[:, 2 * j:2 * j + 2, :])
            for b in range(4):
                vec.wait_ge(lru_exp, b + 1)
                th = rows[:, b // 2, 3072 + 512 * (b % 2):3072 + 512 * (b % 2 + 1)]
                xin = y_t[:, 2 * b:2 * b + 2, :].rearrange("p k s -> p (k s)")
                V.scalar_tensor_tensor(xin, act_tmp[:, b % 2, :], 1.0, xin, ALU.add, ALU.mult).then_inc(lru_in, 1)
                vec.wait_ge(lru_in, b + 1)
                link(V.tensor_scalar(scratch[:, 0:512], th, 1.0, None, ALU.add))
                link(V.reciprocal(scratch[:, 0:512], scratch[:, 0:512]))
                ins = V.tensor_tensor(th, th, scratch[:, 0:512], ALU.mult)
                if b < 3:
                    link(ins)
            ins.then_inc(lru_ratio, 1)
            vec.wait_ge(lru_ratio, 1)
            vec.wait_ge(lru_root, 1)
            chunk_read(vec, "y_lru1")
            chunk_read(vec, "y_lru0")
            for f in range(KT):
                ins = V.tensor_tensor(tile_of(3072, f), tile_of(3072, f), y_t[:, f, :], ALU.mult)
            link(ins)
            for f in range(KT):
                ins = V.tensor_tensor_scan(y_t[:, f, :], h_rows[:, f // 4, S * (f % 4):S * (f % 4 + 1)],
                                           tile_of(3072, f), 0.0, ALU.mult, ALU.add)
            link(ins)
            for f in range(KT):
                ins = V.tensor_tensor(y_t[:, f, :], y_t[:, f, :], tile_of(2048, f), ALU.mult)
            normed.mark(ins, "lru_y", vec)
            for h in range(RET_HEADS):
                i = n_units + h
                score.arrived(vec, i)
                if h >= 2:
                    xpose.arrived(vec, ("ret", h - 2))
                score.freed(V.tensor_tensor(probs_t[:, h % 2, 0:3 * P], psum[:, SCORE_BANK + score.slot(i), 0:3 * P],
                                            L("decay")[:, 3 * P * h:3 * P * (h + 1)], ALU.mult), i, vec)
                V.memset(lam_tmp[:, 7:8], 0.0).then_inc(ret_decayed, 1)
                vec.wait_ge(ret_decayed, h + 1)
            for h in range(RET_HEADS):
                xpose.read(vec, ("ret", h))
            link(V.tensor_scalar(head_sums[:, :, :], head_sums[:, :, :], -1.0 / S, None, ALU.mult))
            for t in range(T):
                o = h_rows[:, t, :].rearrange("p (a h d) -> p a h d", a=1, h=RET_HEADS)
                link(V.tensor_tensor(o[:, 0], o[:, 0], spread(head_sums[:, t, :], [P, RET_HEADS, S], 2), ALU.add))
                sq = scratch[:, :].rearrange("p (h d) -> p h d", d=S)
                link(V.tensor_tensor(sq, o[:, 0], o[:, 0], ALU.mult))
                link(V.tensor_reduce(sumsq[:, 0:RET_HEADS], sq, AX_X, ALU.add))
                r = scale_from(f"gn{t}", sumsq[:, 0:RET_HEADS], S)
                link(V.tensor_tensor(o[:, 0], o[:, 0], spread(r, [P, RET_HEADS, S], 2), ALU.mult))
            for b in range(2):
                for t in range(T):
                    n = 2 * b + t
                    use = (f"g_ret{b}", t)
                    vec.wait_ge(g_tanh, n + 1)
                    dst = rows[:, t, 2048 + 512 * b:2048 + 512 * (b + 1)]
                    proj.freed(V.scalar_tensor_tensor(dst, act_tmp[:, n % 2, :], 1.0, psum[:, PROJ_BANK + proj.slot(use), :],
                                                      ALU.add, ALU.mult), use, vec)
            normed.mark(V.tensor_tensor(h_rows[:, :, :], h_rows[:, :, :], rows[:, :, 2048:3072], ALU.mult), "g_ret", vec)
            for j in range(4):
                xpose.arrived(vec, f"ret_y{j}")
                src = psum[:, XPOSE_BANK + xpose.slot(f"ret_y{j}"), :].rearrange("p (a s) -> p a s", a=2)
                xpose.freed(V.tensor_tensor(pair_of(0, j).rearrange("p (a s) -> p a s", a=2), src,
                                            spread(L("ret_gn")[:, 2 * j:2 * j + 2], [P, 2, S], 2), ALU.mult),
                            f"ret_y{j}", vec)
            for b in range(2):
                for name, gate, c0 in (("ret_o", "gate_r", 1024), ("lru_o", "gate_l", 2048)):
                    for half in range(2):
                        use = (f"{name}{b}", half)
                        proj.arrived(vec, use)
                        proj.read(vec, (f"{gate}{b}", half))
                        part = pair_of(c0, 2 * b + half)
                        proj.freed(V.scalar_tensor_tensor(part, part, 1.0, psum[:, PROJ_BANK + proj.slot(use), :],
                                                          ALU.add, ALU.mult), use, vec)
                for half in range(2):
                    part = pair_of(1024, 2 * b + half)
                    ins = V.tensor_tensor(part, part, pair_of(2048, 2 * b + half), ALU.add)
                if b == 0:
                    link(ins)
            normed.mark(ins, "mix", vec)
            for b in range(2):
                for t in range(T):
                    use = (f"mix_out{b}", t)
                    proj.arrived(vec, use)
                    part = x[:, t, b * CH:(b + 1) * CH]
                    proj.freed(V.scalar_tensor_tensor(part, psum[:, PROJ_BANK + proj.slot(use), :], 0.5, part,
                                                      ALU.mult, ALU.add), use, vec)
            x_ready.mark(V.memset(lam_tmp[:, 7:8], 0.0), "x3", vec)
            norm_rows("x3", x, h_rows)
            for j in range(4):
                turn_in(f"x3_{j}", h_t[:, 2 * j:2 * j + 2, :], L("norm2")[:, 2 * j:2 * j + 2])
            for i in range(FFN_STEPS):
                for half in range(2):
                    use = (f"up_g{i}", half)
                    proj.arrived(vec, use)
                    for lag in range(3):
                        for a in range(2):
                            f = 4 * i + 2 * half + a
                            src = psum[:, PROJ_BANK + proj.slot(use), a * S:(a + 1) * S]
                            dst = rows[:, i % 2, 512 * half + a * S:512 * half + (a + 1) * S]
                            w = L("ffn_conv_w")[:, 3 * f + 2 - lag:3 * f + 3 - lag]
                            if lag == 0:
                                ins = V.tensor_scalar(dst, src, w, L("ffn_conv_b")[:, f:f + 1], ALU.mult, ALU.add)
                            else:
                                ins = V.scalar_tensor_tensor(dst[:, lag:], src[:, 0:S - lag], w, dst[:, lag:],
                                                             ALU.mult, ALU.add)
                        if lag < 2:
                            link(ins)
                    proj.freed(ins, use, vec)
                    V.memset(lam_tmp[:, 7:8], 0.0).then_inc(conv_gate, 1)
                    vec.wait_ge(conv_gate, 2 * i + half + 1)
                for half in range(2):
                    use = (f"up_v{i}", half)
                    proj.arrived(vec, use)
                    vec.wait_ge(conv_gelu, 2 * i + half + 1)
                    if i >= 2:
                        vec.wait_ge(down_done, i - 1)
                    proj.freed(V.tensor_tensor(rows[:, i % 2, 1024 + 512 * half:1024 + 512 * (half + 1)],
                                               psum[:, PROJ_BANK + proj.slot(use), :],
                                               rows[:, i % 2, 512 * half:512 * (half + 1)], ALU.mult), use, vec)
                    V.memset(lam_tmp[:, 7:8], 0.0).then_inc(ffn_ready, 1)
                    vec.wait_ge(ffn_ready, 2 * i + half + 1)
            vec.wait_ge(down_done, FFN_STEPS)
            for t in range(T):
                for half in range(2):
                    part = x[:, t, half * CH:(half + 1) * CH]
                    ins = V.tensor_tensor(part, psum[:, 4 + 2 * t + half, :], part, ALU.add)
            x_ready.mark(ins, "final", vec)
            squares.wait(vec, "final")
            r = scale_from("final", x_sums[:, squares.names.index("final"), :], D)
            for t in range(T):
                ins = V.scalar_tensor_tensor(h_rows[:, t, :], x[:, t, :], r[:, t:t + 1], L("norm_f"), ALU.mult, ALU.mult)
            ins.then_inc(out_ready, 1)


def layout(inputs):
    f = {k: np.asarray(v) for k, v in inputs.items()}
    zeros = lambda n: np.zeros((P, n), np.float32)
    cols = lambda v: np.ascontiguousarray(v.reshape(-1, P).T)
    bc = lambda v: np.broadcast_to(v.reshape(1, -1), (P, v.size))

    def rope_tables(pos, half, theta):
        inv = np.float32(theta) ** (-np.arange(half, dtype=np.float32) / np.float32(half))
        ang = pos.astype(np.float32)[:, None] * inv[None, :].astype(np.float32)
        return np.cos(ang).astype(np.float32), np.sin(ang).astype(np.float32)

    def by_token(a):
        return np.ascontiguousarray(a.reshape(T, P, -1).transpose(1, 0, 2)).reshape(P, -1)

    q, k = np.arange(P)[:, None], np.arange(P)[None, :]
    above = np.where(k > q, np.float32(FAR), np.float32(0))
    pos = np.arange(S)
    cos0, sin0 = rope_tables(pos, 4, 500000.0)
    cos1, sin1 = rope_tables(pos, 8, 500000.0)
    ends = 16 * np.arange(N_CMP) + 31
    cosc, sinc = rope_tables(ends, 8, 500000.0)
    padded = lambda a: np.concatenate([a, np.zeros((P - len(a), a.shape[1]), np.float32)])
    cmp_far = np.full((S, 16), FAR, np.float32)
    cmp_far[:, :N_CMP] = np.where(ends[None, :] <= pos[:, None], 0, FAR)
    log_gamma = np.log1p(-np.exp2(-5.0 - np.arange(RET_HEADS)))
    i, j = np.arange(S)[None, :], np.arange(S)[:, None]
    decay = np.exp(log_gamma[:, None, None] * np.abs(i - j)) * (j // 64 <= i // 64)
    decay = decay * 128 ** -0.5
    decay_parts = np.concatenate([decay[:, 0:P, :], decay[:, P:, P:]], axis=2)
    e = {"ident": np.eye(P, dtype=np.float32), "causal": np.concatenate([above, zeros(P), above], 1),
         "tril_t": (q <= k).astype(np.float32), "cos0": by_token(cos0), "sin0": by_token(sin0),
         "cos1": by_token(cos1), "sin1": by_token(sin1), "cos_cmp": padded(cosc), "sin_cmp": padded(sinc),
         "cmp_mask": by_token(cmp_far), "cmp_valid": by_token((pos >= 31).astype(np.float32)[:, None]),
         "mem_norm": cols(f["mem_norm"]), "l0_norm": cols(f["l0_norm"]), "l1_norm": cols(f["l1_norm"]),
         "a_vnorm": bc(f["l0_a_vnorm"]), "a_bs": f["l0_a_bs"].T,
         "a_ws_t": f["l0_a_ws"].transpose(2, 0, 1).reshape(P, -1),
         "b_subln": bc(f["l0_b_subln"]), "c_norm": bc(f["l1_c_norm"]),
         "conv_w": f["l1_c_conv_w"].T.reshape(4, P, 31).transpose(1, 0, 2).reshape(P, -1),
         "conv_b": cols(f["l1_c_conv_b"]), "d_qnorm": bc(f["l1_d_qnorm"]), "d_knorm": bc(f["l1_d_knorm"]),
         "cmp_pos": np.concatenate([f["l1_d_cmp_pos_k"].T, f["l1_d_cmp_pos_v"].T]),
         "cmp_w2": np.concatenate([f["l1_d_cmp_w2_k"], f["l1_d_cmp_w2_v"]], 1),
         "inv_freq": bc((np.float32(10000.0) ** (-np.arange(64, dtype=np.float32) / np.float32(64))))}
    for n in ("b_qnorm", "b_knorm", "b_lq1", "b_lk1", "b_lq2", "b_lk2"):
        e[n] = bc(f["l0_" + n])
    for l in range(2):
        e[f"m{l}_qnorm"], e[f"m{l}_knorm"] = bc(f[f"l{l}_m_qnorm"]), bc(f[f"l{l}_m_knorm"])
    taps = lambda w, n: w.T.reshape(-1, P, n).transpose(1, 0, 2).reshape(P, -1)
    late = {"norm1": cols(f["norm1_w_2"]), "decay": decay_parts.transpose(1, 0, 2).reshape(P, -1).astype(np.float32),
            "ret_gn": cols(f["ret_gn_w_2"]), "merge_b": cols(f["merge_gate_b_2"]),
            "lru_conv_w": taps(f["lru_conv_w_2"][0], 4), "lru_conv_b": cols(f["lru_conv_b_2"]),
            "lru_b_r": cols(f["lru_b_r_2"]), "lru_b_i": cols(f["lru_b_i_2"]), "lru_lambda": cols(f["lru_lambda_2"]),
            "norm2": cols(f["norm2_w_2"]), "ffn_conv_w": taps(f["ffn_conv_w_2"][0], 3),
            "ffn_conv_b": cols(f["ffn_conv_b_2"]), "norm_f": bc(f["norm_f_w_2"])}
    pack = lambda spec, parts: np.concatenate([parts[n].reshape(P, w) for n, w in spec], 1)

    def block(w):
        k, n = w.shape
        if k == D and n < CH:
            w, n = np.concatenate([w, np.zeros((k, CH - n), np.float32)], 1), CH
        out = np.zeros((P, BLK), np.float32)
        out[:, :(k // P) * n] = w.reshape(k // P, P, n).transpose(1, 0, 2).reshape(P, -1)
        return out

    w0, w_out = f["l0_w_in"], f["l0_w_out"]
    blocks = {"kv0": f["l0_m_wkv"], "kv1": f["l1_m_wkv"], "a_u": w0[:, 0:512], "a_v": w0[:, 512:1024],
              "a_g": w0[:, 1024:1536], "b_q": w0[:, 1536:2048], "b_k": w0[:, 2048:2560], "b_v": w0[:, 2560:3072],
              "b_g": w0[:, 3072:3584], "m_qg0": w0[:, 3584:4096]}
    w1 = f["l1_w_in"]
    kv = lambda j: w1[:, 2048 + 64 * j:2048 + 64 * (j + 1)]
    blocks.update({
        "c_a": w1[:, 0:512], "c_b": w1[:, 512:1024], "c_g": w1[:, 1024:1536], "d_q": w1[:, 1536:2048],
        "dkv1": np.concatenate([kv(j) for j in (0, 2, 1, 3, 4, 5, 8, 9)], 1),
        "dkv2": np.concatenate([kv(j) for j in (6, 7, 10, 11)] + [w1[:, 2816:2840]], 1),
        "d_g": w1[:, 2840:3352], "m_qg1": w1[:, 3352:3864]})
    cmp_w1 = np.concatenate([f["l1_d_cmp_w1_" + n].reshape(32, 64, P).transpose(1, 0, 2).reshape(64, -1)
                             for n in "kv"])
    w2 = f["w_in_2"][0]
    for n, at in (("r_q", 0), ("r_k", 512), ("r_v0", 1024), ("r_v1", 1536), ("g_ret0", 2048), ("g_ret1", 2560),
                  ("x_lru0", 3072), ("x_lru1", 3584), ("y_lru0", 4096), ("y_lru1", 4608), ("gate_r0", 5120),
                  ("gate_r1", 5632), ("gate_l0", 6144), ("gate_l1", 6656)):
        blocks[n] = w2[:, at:at + CH]
    for b in range(2):
        for n, w in (("ret_o", "w_ret_o_2"), ("lru_o", "w_lru_o_2"), ("mix_out", "w_out_2")):
            blocks[f"{n}{b}"] = f[w][0][:, b * CH:(b + 1) * CH]
    for i in range(FFN_STEPS):
        blocks[f"up_g{i}"] = f["ffn_w_up_2"][0][:, i * CH:(i + 1) * CH]
        blocks[f"up_v{i}"] = f["ffn_w_up_2"][0][:, FFN_STEPS * CH + i * CH:FFN_STEPS * CH + (i + 1) * CH]
        blocks[f"down{i}"] = f["ffn_w_down_2"][0][i * CH:(i + 1) * CH]
    lru_w = np.concatenate([f[n][0].reshape(4, 2, P, S).transpose(2, 0, 1, 3).reshape(P, -1)
                            for n in ("lru_w_r_2", "lru_w_i_2")], 1)
    ready = {"cmp_w1": cmp_w1, "lru_w": lru_w}
    for l in range(2):
        w = f[f"l{l}_w_out"]
        blocks[f"out{l}_r"], blocks[f"out{l}_a"], blocks[f"out{l}_b"] = w[D:], w[:D, 0:CH], w[:D, CH:]
    return {"early": pack(EARLY, e), "late": pack(LATE, late),
            "blocks": np.stack([ready[n] if n in ready else block(blocks[n]) for n, _ in BLOCKS]),
            "x": f["x"].reshape(S, D), "mem": f["mem"].reshape(S, D),
            "positions": np.ascontiguousarray(f["positions_2"].reshape(T, P).T)}


def kernel(**inputs):
    import concourse.bacc as bacc
    from concourse.bass_utils import run_bass_kernel_spmd

    arrays = layout(inputs)
    nc = bacc.Bacc("TRN2", target_bir_lowering=False, num_devices=1)
    aps = {n: nc.dram_tensor(f"in_{n}", a.shape, mybir.dt.from_np(a.dtype), kind="ExternalInput").ap()
           for n, a in arrays.items()}
    out = nc.dram_tensor("out_x", (S, D), F32, kind="ExternalOutput").ap()
    build(nc, aps["early"], aps["late"], aps["positions"], aps["x"], aps["mem"], aps["blocks"], out)
    r = run_bass_kernel_spmd(nc, [{f"in_{n}": a for n, a in arrays.items()}], core_ids=[0])
    return r.results[0]["out_x"].reshape(1, S, D)
```
